# Optimizing a Trainium2 kernel written in Bass

```python
import math
import jax, jax.numpy as jnp
from jax import lax
import numpy as np

'''One inference step (DEPTH layers) of a hybrid decoder built from parallel head groups.

Each layer:
  RMSNorm -> one combined input projection whose columns are split into
    [S5 channels (SSM_WIDTH) | q (ATTN_WIDTH) | k (ATTN_WIDTH) | v (ATTN_WIDTH)]
  S5 head group: N_SSM_GROUPS groups of 16 channels, each group drives one 64-dim
    complex diagonal state (ZOH, per-group step), associative scan over positions,
    y = Re(C x) + D u, then GELU and a GLU.
  Attention head group: N_HEADS heads of HEAD_DIM, rotary q/k, dilated sliding-window
    attention with (window, dilation) in (128,1), (512,4), (2048,16): each query reads
    positions t, t-d, t-2d, ..., t-window; the three branch outputs are merged per
    position and head with weights proportional to their softmax denominators.
  Per-group RMSNorm, concat, one output projection, residual add.
  RMSNorm -> hierarchical MoE (top-1 of 4 expert groups, then top-2 of 8 SwiGLU
    experts inside it) -> residual add.
Final RMSNorm.

Inputs:
  x_prompt (BATCH, SEQ, D_MODEL), positions 0..SEQ-1
  x_sample (DEC_BATCH, DEC_SEQ, D_MODEL), positions PAST_LEN..PAST_LEN+DEC_SEQ-1
  cache_k, cache_v (DEPTH, DEC_BATCH, min(2048, PAST_LEN), N_HEADS, HEAD_DIM):
    rotated keys / values of the last min(2048, PAST_LEN) past positions, oldest first
  state_ssm_re, state_ssm_im (DEPTH, DEC_BATCH, N_SSM_GROUPS, SSM_STATE)
Returns the tuple
  (y_prompt (BATCH, SEQ, D_MODEL),
   y_sample (DEC_BATCH, DEC_SEQ, D_MODEL),
   new_k_prompt, new_v_prompt (DEPTH, BATCH, min(2048, SEQ), N_HEADS, HEAD_DIM),
   new_ssm_re_prompt, new_ssm_im_prompt (DEPTH, BATCH, N_SSM_GROUPS, SSM_STATE),
   new_k_sample, new_v_sample (DEPTH, DEC_BATCH, DEC_SEQ, N_HEADS, HEAD_DIM),
   new_ssm_re_sample, new_ssm_im_sample (DEPTH, DEC_BATCH, N_SSM_GROUPS, SSM_STATE))
'''

D_MODEL = 2048
BATCH = 1
SEQ = 512
DEPTH = 1
DEC_BATCH = 8
DEC_SEQ = 1
PAST_LEN = 1024
PAGE_SIZE = 128

MIX_WIDTH = D_MODEL
SSM_WIDTH = MIX_WIDTH // 2
ATTN_WIDTH = MIX_WIDTH - SSM_WIDTH
SSM_GROUP = 16
N_SSM_GROUPS = SSM_WIDTH // SSM_GROUP
SSM_STATE = 64
HEAD_DIM = 128
N_HEADS = ATTN_WIDTH // HEAD_DIM
D_IN = SSM_WIDTH + 3 * ATTN_WIDTH
DILATED_BRANCHES = ((128, 1), (512, 4), (2048, 16))
MAX_WINDOW = 2048
ROPE_THETA = 10000.0
N_EXPERT_GROUPS = 4
EXPERTS_PER_GROUP = 8
N_EXPERTS = N_EXPERT_GROUPS * EXPERTS_PER_GROUP
TOP_K = 2
EXPERT_FF = 512
MOE_BLOCK = 64
NORM_EPS = 1e-6

kernel_name = 'hymba_s5_dilated_hmoe_step'

F32 = jnp.float32

def _rmsnorm(x, g):
    xf = x.astype(F32)
    y = xf * lax.rsqrt(jnp.mean(xf * xf, axis=-1, keepdims=True) + NORM_EPS) * g.astype(F32)
    return y.astype(x.dtype)

def _rope(x, pos):
    half = x.shape[-1] // 2
    inv = ROPE_THETA ** (-jnp.arange(half, dtype=F32) / half)
    ang = pos[:, None] * inv[None, :]
    cos = jnp.cos(ang)[None, :, None, :]
    sin = jnp.sin(ang)[None, :, None, :]
    xf = x.astype(F32)
    x1, x2 = xf[..., :half], xf[..., half:]
    return jnp.concatenate([x1 * cos - x2 * sin, x2 * cos + x1 * sin], axis=-1).astype(x.dtype)

def _mixer_inputs(x, g_norm, w_in, pos):
    b, s, _ = x.shape
    h = _rmsnorm(x, g_norm)
    proj = h @ w_in
    u, q, k, v = jnp.split(proj, [SSM_WIDTH, SSM_WIDTH + ATTN_WIDTH, SSM_WIDTH + 2 * ATTN_WIDTH], axis=-1)
    u = u.reshape(b, s, N_SSM_GROUPS, SSM_GROUP)
    q = _rope(q.reshape(b, s, N_HEADS, HEAD_DIM), pos)
    k = _rope(k.reshape(b, s, N_HEADS, HEAD_DIM), pos)
    v = v.reshape(b, s, N_HEADS, HEAD_DIM)
    return u, q, k, v

def _s5(u, x0_re, x0_im, a_re, a_im, log_dt, b_re, b_im, c_re, c_im, d_skip):
    uf = u.astype(F32)
    lam = lax.complex(a_re.astype(F32), a_im.astype(F32))
    dt = jnp.exp(log_dt.astype(F32))[:, None]
    lam_bar = jnp.exp(lam * dt)
    b_c = lax.complex(b_re.astype(F32), b_im.astype(F32))
    b_bar = ((lam_bar - 1.0) / lam)[..., None] * b_c
    bu = jnp.einsum('bsgp,gnp->bsgn', uf, b_bar)
    x0 = lax.complex(x0_re.astype(F32), x0_im.astype(F32))
    bu = bu.at[:, 0].add(lam_bar * x0)
    a = jnp.broadcast_to(lam_bar, bu.shape)

    def combine(left, right):
        a1, b1 = left
        a2, b2 = right
        return a1 * a2, a2 * b1 + b2

    _, xs = lax.associative_scan(combine, (a, bu), axis=1)
    c_c = lax.complex(c_re.astype(F32), c_im.astype(F32))
    y = jnp.einsum('gpn,bsgn->bsgp', c_c, xs).real + d_skip.astype(F32) * uf
    x_last = xs[:, -1]
    return y, x_last.real, x_last.imag

def _ssm_branch(u, x0_re, x0_im, lp):
    b, s = u.shape[:2]
    y, sr, si = _s5(u, x0_re, x0_im, lp['ssm_a_re'], lp['ssm_a_im'], lp['ssm_log_dt'],
                    lp['ssm_b_re'], lp['ssm_b_im'], lp['ssm_c_re'], lp['ssm_c_im'], lp['ssm_d'])
    z = jax.nn.gelu(y.reshape(b, s, SSM_WIDTH)).astype(u.dtype)
    z = z * jax.nn.sigmoid(z @ lp['w_glu'])
    return z, sr, si

def _branch_prompt(q, k, v, window, dilation):
    b, s, h, dh = q.shape
    n = window // dilation
    qb = n
    nb = -(-s // (dilation * qb))
    sp = nb * qb * dilation

    def strided(t):
        t = jnp.pad(t, ((0, 0), (0, sp - s), (0, 0), (0, 0)))
        t = t.reshape(b, nb * qb, dilation, h, dh).transpose(0, 2, 1, 3, 4)
        return t.reshape(b, dilation, nb, qb, h, dh)

    def with_prev(t):
        prev = jnp.pad(t[:, :, :-1], ((0, 0), (0, 0), (1, 0), (0, 0), (0, 0), (0, 0)))
        return jnp.concatenate([prev, t], axis=3)

    qs = strided(q)
    kb = with_prev(strided(k))
    vb = with_prev(strided(v))
    scores = jnp.einsum('brnqhc,brnkhc->brnhqk', qs, kb, preferred_element_type=F32) * (dh ** -0.5)
    qi = jnp.arange(qb)[:, None]
    ki = jnp.arange(2 * qb)[None, :]
    dist = qi + qb - ki
    band = (dist >= 0) & (dist <= n)
    has_prev = (jnp.arange(nb) > 0)[:, None, None] | (ki >= qb)[None]
    mask = band[None] & has_prev
    scores = jnp.where(mask[None, None, :, None], scores, -jnp.inf)
    m = jnp.max(scores, axis=-1, keepdims=True)
    p = jnp.exp(scores - m)
    l = jnp.sum(p, axis=-1, keepdims=True)
    o = jnp.einsum('brnhqk,brnkhc->brnqhc', p / l, vb.astype(F32))
    lse = (m + jnp.log(l))[..., 0]
    o = o.reshape(b, dilation, nb * qb, h, dh).transpose(0, 2, 1, 3, 4).reshape(b, sp, h, dh)[:, :s]
    lse = lse.transpose(0, 1, 2, 4, 3).reshape(b, dilation, nb * qb, h)
    lse = lse.transpose(0, 2, 1, 3).reshape(b, sp, h)[:, :s]
    return o, lse

def _branch_sample(q, k_all, v_all, window, dilation, n_past):
    t = q.shape[1]
    dh = q.shape[-1]
    n = window // dilation
    idx = (n_past + jnp.arange(t))[:, None] - dilation * jnp.arange(n + 1)[None, :]
    valid = idx >= 0
    idx = jnp.maximum(idx, 0)
    kg = k_all[:, idx]
    vg = v_all[:, idx]
    scores = jnp.einsum('bthc,btjhc->bthj', q, kg, preferred_element_type=F32) * (dh ** -0.5)
    scores = jnp.where(valid[None, :, None, :], scores, -jnp.inf)
    m = jnp.max(scores, axis=-1, keepdims=True)
    p = jnp.exp(scores - m)
    l = jnp.sum(p, axis=-1, keepdims=True)
    o = jnp.einsum('bthj,btjhc->bthc', p / l, vg.astype(F32))
    lse = (m + jnp.log(l))[..., 0]
    return o, lse

def _merge_branches(outs, lses):
    alpha = jax.nn.softmax(jnp.stack(lses, axis=0), axis=0)
    return jnp.sum(alpha[..., None] * jnp.stack(outs, axis=0), axis=0)

def _hier_moe(h, w_rg, b_rg, w_re, b_re, w_g, w_u, w_d):
    t, d = h.shape
    hf = h.astype(F32)
    lg = hf @ w_rg.astype(F32) + b_rg.astype(F32)
    pg = jax.nn.softmax(lg, axis=-1)
    grp = jnp.argmax(lg, axis=-1)
    gate1 = jnp.take_along_axis(pg, grp[:, None], axis=-1)
    le = jnp.einsum('td,dge->tge', hf, w_re.astype(F32)) + b_re.astype(F32)
    le = jnp.take_along_axis(le, grp[:, None, None], axis=1)[:, 0]
    top_v, top_i = lax.top_k(le, TOP_K)
    gates = gate1 * jax.nn.softmax(top_v, axis=-1)
    eid = grp[:, None] * EXPERTS_PER_GROUP + top_i
    tk = t * TOP_K
    e_flat = eid.reshape(tk)
    w_flat = gates.reshape(tk)
    tok_flat = jnp.repeat(jnp.arange(t, dtype=jnp.int32), TOP_K)
    order = jnp.argsort(e_flat)
    e_s, tok_s, w_s = e_flat[order], tok_flat[order], w_flat[order]
    counts = jnp.bincount(e_flat, length=N_EXPERTS)
    padded = (counts + MOE_BLOCK - 1) // MOE_BLOCK * MOE_BLOCK
    off = jnp.cumsum(counts) - counts
    pend = jnp.cumsum(padded)
    poff = pend - padded
    dest = poff[e_s] + jnp.arange(tk) - off[e_s]
    n_blocks = -(-tk // MOE_BLOCK) + N_EXPERTS
    n_rows = n_blocks * MOE_BLOCK
    row_tok = jnp.full((n_rows,), t, jnp.int32).at[dest].set(tok_s)
    block_e = jnp.minimum(jnp.searchsorted(pend, jnp.arange(n_blocks) * MOE_BLOCK, side='right'), N_EXPERTS - 1)
    h_pad = jnp.concatenate([h, jnp.zeros((1, d), h.dtype)], axis=0)

    def expert_block(args):
        rows, e = args
        xb = h_pad[rows]
        return (jax.nn.silu(xb @ w_g[e]) * (xb @ w_u[e])) @ w_d[e]

    y_rows = lax.map(expert_block, (row_tok.reshape(n_blocks, MOE_BLOCK), block_e)).reshape(n_rows, d)
    contrib = y_rows[dest].astype(F32) * w_s[:, None]
    out = jax.ops.segment_sum(contrib, tok_s, num_segments=t)
    return out.astype(h.dtype)

def _finish(x, z_ssm, o_attn, lp):
    b, s, _ = x.shape
    mix = jnp.concatenate([_rmsnorm(z_ssm, lp['g_ssm_out']),
                           _rmsnorm(o_attn.reshape(b, s, ATTN_WIDTH), lp['g_attn_out'])], axis=-1)
    x = x + mix @ lp['w_out']
    h = _rmsnorm(x, lp['g_ffn_norm'])
    y = _hier_moe(h.reshape(b * s, D_MODEL), lp['w_router_group'], lp['b_router_group'],
                  lp['w_router_expert'], lp['b_router_expert'],
                  lp['w_expert_gate'], lp['w_expert_up'], lp['w_expert_down'])
    return x + y.reshape(b, s, D_MODEL)

def _layer_prompt(x, lp):
    b, s, _ = x.shape
    pos = jnp.arange(s, dtype=F32)
    u, q, k, v = _mixer_inputs(x, lp['g_mix_norm'], lp['w_in'], pos)
    zeros = jnp.zeros((b, N_SSM_GROUPS, SSM_STATE), F32)
    z, sr, si = _ssm_branch(u, zeros, zeros, lp)
    outs, lses = [], []
    for window, dilation in DILATED_BRANCHES:
        o_i, l_i = _branch_prompt(q, k, v, window, dilation)
        outs.append(o_i)
        lses.append(l_i)
    o = _merge_branches(outs, lses).astype(x.dtype)
    x = _finish(x, z, o, lp)
    wb = min(MAX_WINDOW, s)
    return x, k[:, s - wb:], v[:, s - wb:], sr, si

def _layer_sample(x, k_past, v_past, sr0, si0, lp):
    b, t, _ = x.shape
    pos = PAST_LEN + jnp.arange(t, dtype=F32)
    u, q, k, v = _mixer_inputs(x, lp['g_mix_norm'], lp['w_in'], pos)
    z, sr, si = _ssm_branch(u, sr0, si0, lp)
    k_all = jnp.concatenate([k_past.astype(k.dtype), k], axis=1)
    v_all = jnp.concatenate([v_past.astype(v.dtype), v], axis=1)
    n_past = k_past.shape[1]
    outs, lses = [], []
    for window, dilation in DILATED_BRANCHES:
        o_i, l_i = _branch_sample(q, k_all, v_all, window, dilation, n_past)
        outs.append(o_i)
        lses.append(l_i)
    o = _merge_branches(outs, lses).astype(x.dtype)
    x = _finish(x, z, o, lp)
    return x, k, v, sr, si

def setup_inputs(seed: int = 0) -> dict:
    key = jax.random.key(seed)
    ks = jax.random.split(key, 32)

    def nrm(k, shape, std):
        return std * jax.random.normal(k, shape, F32)

    wb = min(MAX_WINDOW, PAST_LEN)
    g, n, p = N_SSM_GROUPS, SSM_STATE, SSM_GROUP
    return {
        'x_prompt': nrm(ks[0], (BATCH, SEQ, D_MODEL), 1.0),
        'x_sample': nrm(ks[1], (DEC_BATCH, DEC_SEQ, D_MODEL), 1.0),
        'cache_k': nrm(ks[2], (DEPTH, DEC_BATCH, wb, N_HEADS, HEAD_DIM), 1.0),
        'cache_v': nrm(ks[3], (DEPTH, DEC_BATCH, wb, N_HEADS, HEAD_DIM), 1.0),
        'state_ssm_re': nrm(ks[4], (DEPTH, DEC_BATCH, g, n), 0.5),
        'state_ssm_im': nrm(ks[5], (DEPTH, DEC_BATCH, g, n), 0.5),
        'g_mix_norm': 1.0 + nrm(ks[6], (DEPTH, D_MODEL), 0.02),
        'w_in': nrm(ks[7], (DEPTH, D_MODEL, D_IN), D_MODEL ** -0.5),
        'ssm_a_re': -0.5 + nrm(ks[8], (DEPTH, g, n), 0.01),
        'ssm_a_im': jnp.pi * jnp.arange(n, dtype=F32) + nrm(ks[9], (DEPTH, g, n), 0.01),
        'ssm_log_dt': jax.random.uniform(ks[10], (DEPTH, g), F32, minval=math.log(1e-3), maxval=math.log(1e-1)),
        'ssm_b_re': nrm(ks[11], (DEPTH, g, n, p), (2 * p) ** -0.5),
        'ssm_b_im': nrm(ks[12], (DEPTH, g, n, p), (2 * p) ** -0.5),
        'ssm_c_re': nrm(ks[13], (DEPTH, g, p, n), (2 * n) ** -0.5),
        'ssm_c_im': nrm(ks[14], (DEPTH, g, p, n), (2 * n) ** -0.5),
        'ssm_d': nrm(ks[15], (DEPTH, g, p), 1.0),
        'w_glu': nrm(ks[16], (DEPTH, SSM_WIDTH, SSM_WIDTH), SSM_WIDTH ** -0.5),
        'g_ssm_out': 1.0 + nrm(ks[17], (DEPTH, SSM_WIDTH), 0.02),
        'g_attn_out': 1.0 + nrm(ks[18], (DEPTH, ATTN_WIDTH), 0.02),
        'w_out': nrm(ks[19], (DEPTH, MIX_WIDTH, D_MODEL), MIX_WIDTH ** -0.5),
        'g_ffn_norm': 1.0 + nrm(ks[20], (DEPTH, D_MODEL), 0.02),
        'w_router_group': nrm(ks[21], (DEPTH, D_MODEL, N_EXPERT_GROUPS), D_MODEL ** -0.5),
        'b_router_group': nrm(ks[22], (DEPTH, N_EXPERT_GROUPS), 0.01),
        'w_router_expert': nrm(ks[23], (DEPTH, D_MODEL, N_EXPERT_GROUPS, EXPERTS_PER_GROUP), D_MODEL ** -0.5),
        'b_router_expert': nrm(ks[24], (DEPTH, N_EXPERT_GROUPS, EXPERTS_PER_GROUP), 0.01),
        'w_expert_gate': nrm(ks[25], (DEPTH, N_EXPERTS, D_MODEL, EXPERT_FF), D_MODEL ** -0.5),
        'w_expert_up': nrm(ks[26], (DEPTH, N_EXPERTS, D_MODEL, EXPERT_FF), D_MODEL ** -0.5),
        'w_expert_down': nrm(ks[27], (DEPTH, N_EXPERTS, EXPERT_FF, D_MODEL), EXPERT_FF ** -0.5),
        'g_final': 1.0 + nrm(ks[28], (D_MODEL,), 0.02),
    }

def reference(x_prompt, x_sample, cache_k, cache_v, state_ssm_re, state_ssm_im,
              g_mix_norm, w_in, ssm_a_re, ssm_a_im, ssm_log_dt, ssm_b_re, ssm_b_im,
              ssm_c_re, ssm_c_im, ssm_d, w_glu, g_ssm_out, g_attn_out, w_out, g_ffn_norm,
              w_router_group, b_router_group, w_router_expert, b_router_expert,
              w_expert_gate, w_expert_up, w_expert_down, g_final):
    xp, xs = x_prompt, x_sample
    kp_l, vp_l, srp_l, sip_l = [], [], [], []
    ks_l, vs_l, srs_l, sis_l = [], [], [], []
    for l in range(DEPTH):
        lp = {
            'g_mix_norm': g_mix_norm[l], 'w_in': w_in[l],
            'ssm_a_re': ssm_a_re[l], 'ssm_a_im': ssm_a_im[l], 'ssm_log_dt': ssm_log_dt[l],
            'ssm_b_re': ssm_b_re[l], 'ssm_b_im': ssm_b_im[l],
            'ssm_c_re': ssm_c_re[l], 'ssm_c_im': ssm_c_im[l], 'ssm_d': ssm_d[l],
            'w_glu': w_glu[l], 'g_ssm_out': g_ssm_out[l], 'g_attn_out': g_attn_out[l],
            'w_out': w_out[l], 'g_ffn_norm': g_ffn_norm[l],
            'w_router_group': w_router_group[l], 'b_router_group': b_router_group[l],
            'w_router_expert': w_router_expert[l], 'b_router_expert': b_router_expert[l],
            'w_expert_gate': w_expert_gate[l], 'w_expert_up': w_expert_up[l],
            'w_expert_down': w_expert_down[l],
        }
        xp, kp, vp, srp, sip = _layer_prompt(xp, lp)
        xs, kn, vn, srs, sis = _layer_sample(xs, cache_k[l], cache_v[l], state_ssm_re[l], state_ssm_im[l], lp)
        kp_l.append(kp); vp_l.append(vp); srp_l.append(srp); sip_l.append(sip)
        ks_l.append(kn); vs_l.append(vn); srs_l.append(srs); sis_l.append(sis)
    y_prompt = _rmsnorm(xp, g_final)
    y_sample = _rmsnorm(xs, g_final)
    new_k_prompt = jnp.stack(kp_l, axis=0)
    new_v_prompt = jnp.stack(vp_l, axis=0)
    new_ssm_re_prompt = jnp.stack(srp_l, axis=0)
    new_ssm_im_prompt = jnp.stack(sip_l, axis=0)
    new_k_sample = jnp.stack(ks_l, axis=0)
    new_v_sample = jnp.stack(vs_l, axis=0)
    new_ssm_re_sample = jnp.stack(srs_l, axis=0)
    new_ssm_im_sample = jnp.stack(sis_l, axis=0)
    return (y_prompt, y_sample, new_k_prompt, new_v_prompt, new_ssm_re_prompt, new_ssm_im_prompt,
            new_k_sample, new_v_sample, new_ssm_re_sample, new_ssm_im_sample)


_drawn_inputs = setup_inputs


def setup_inputs(seed=0):
    import zlib

    import numpy as np

    out = dict(_drawn_inputs(seed))
    spreads = {}
    factors = {'ssm_a_re': 14.276,
     'g_ssm_out': 12.779,
     'g_attn_out': 13.418,
     'b_router_group': 20.868,
     'b_router_expert': 25.441,
     'g_final': 7.398,
     'g_ffn_norm': 5.526}
    for name, (base, spread) in spreads.items():
        noise = np.random.default_rng([zlib.crc32(name.encode()), seed]).standard_normal(out[name].shape)
        drawn = base * np.exp(spread * noise) if base else spread * noise
        out[name] = __import__('jax').numpy.asarray(drawn.astype(out[name].dtype))
    for name, factor in factors.items():
        out[name] = (out[name] * factor).astype(out[name].dtype)
    return out
```

```python
from contextlib import ExitStack

import concourse.bass as bass
from concourse import mybir

F32 = mybir.dt.float32
F16 = mybir.dt.float16
U32 = mybir.dt.uint32
ALU = mybir.AluOpType
ACT = mybir.ActivationFunctionType
X = mybir.AxisListType.X

P = 128
DM = 2048
KT_D = DM // P
SEQ, NS = 512, 8
T = SEQ + NS
HALF = T // 2
NH, DH = 8, 128
PAIRS = 32
CHUNK = 4
NCH = SEQ // CHUNK
KEYS = 256
NE, EPG, NG, FF = 32, 8, 4, 512
CAP = 96
MAXB = -(-T // CAP)
NOV = (2 * T) // CAP
NBLK = NE + NOV
LISTG = 7
EPS = 1e-6
SCALE = DH ** -0.5
MAGIC = 12582912.0
PI = 3.14159265358979
TWO_PI = (6.28125, 0.0019350051879882812, 3.019916e-07)
BIG = 4096.0


def layout():
    at, off = {}, 0
    for name, n in (("ident", P), ("ones", P), ("rstd", T), ("cos", T), ("sin", T), ("gmix", 16), ("gso", 8),
                    ("gao", 8), ("gffn", 16), ("dskip", 8), ("lr", 64), ("li", 64), ("lamp", 64), ("coef", 64),
                    ("prod", 64), ("vsamp", 64), ("eps", 1), ("stat", 64), ("upper", P)):
        at[name] = off
        off += n
    off = 2600
    for name, n in (("A", 16 * T), ("R", 11664), ("W", 4096), ("U", 8 * T), ("Q", 8 * T), ("K", 8 * T),
                    ("V", 8 * T), ("X", 9792)):
        at[name] = off
        off += n
    at["end"] = off
    return at


def build(nc, t):
    at = layout()
    ctx = ExitStack()
    with ctx:
        arena_t = ctx.enter_context(nc.sbuf_tensor("arena", [P, at["end"]], F32))
        psum_t = ctx.enter_context(nc.psum_tensor("psum", [P, 8 * 512], F32))
        arena = arena_t[:, :]
        ps = psum_t[:, :].rearrange("p (b n) -> p b n", b=8)

        def sem(name):
            return ctx.enter_context(nc.semaphore(name))

        def view(off, n):
            return arena[:, off:off + n]

        def region(name, n, shift=0):
            return view(at[name] + shift, n)

        def dram(name, shape):
            return nc.dram_tensor(name, shape, F32, kind="Internal").ap()

        h_rows = dram("h_rows", (T, DM))
        x2_rows = dram("x2_rows", (T, DM))
        y_rows = dram("y_rows", (2 * T, DM))

        ident, ones = region("ident", P), region("ones", P)
        rstd, cos, sin = region("rstd", T), region("cos", T), region("sin", T)
        gmix, gso, gao, gffn = region("gmix", 16), region("gso", 8), region("gao", 8), region("gffn", 16)
        dskip = region("dskip", 8)
        lam_same = region("lr", 64).rearrange("p (r i) -> p r i", r=2)
        lam_cross = region("li", 64).rearrange("p (r i) -> p r i", r=2)
        lamp = region("lamp", 64).rearrange("p (r i) -> p r i", r=2)
        coef = region("coef", 64).rearrange("p (r i) -> p r i", r=2)
        prod, vsamp = region("prod", 64), region("vsamp", 64)
        eps = region("eps", 1)
        xg = region("A", 16 * T).rearrange("p (k n) -> p k n", k=16)
        wring = region("W", 4096).rearrange("p (s k n) -> p s k n", s=2, k=16)
        u = region("U", 8 * T).rearrange("p (c n) -> p c n", c=8)
        q = region("Q", 8 * T).rearrange("p (c n) -> p c n", c=8)
        k = region("K", 8 * T).rearrange("p (c n) -> p c n", c=8)
        v = region("V", 8 * T).rearrange("p (c n) -> p c n", c=8)
        xs = region("X", 64 * (NCH + 1)).rearrange("p (r i n) -> p r i n", r=2, i=PAIRS)
        x0s = region("X", 512, 8256).rearrange("p (r i n) -> p r i n", r=2, i=PAIRS)
        xns = region("X", 512, 8768).rearrange("p (r i n) -> p r i n", r=2, i=PAIRS)
        sq = region("X", 4160).rearrange("p (s k n) -> p s k n", s=2, k=4)
        braw = region("X", 2048, 4160).rearrange("p (r n) -> p r n", r=2)
        bw = region("Q", 8192).rearrange("p (k r c n) -> p k r c n", k=CHUNK, r=2, c=8)
        NP = 1056
        par = region("R", 3 * NP).rearrange("p (a n) -> p a n", a=3)
        tmp = [region("R", NP, (3 + j) * NP) for j in range(8)] + [region("V", NP, j * NP) for j in range(3)]
        lre, lim, cre, cim = tmp[0], tmp[1], tmp[2], tmp[3]
        rope_in = region("R", 4 * T).rearrange("p (s r n) -> p s r n", s=2, r=2)
        rope_t = region("R", 2 * T, 4 * T).rearrange("p (s n) -> p s n", s=2)
        cosr, sinr = region("R", T, 6 * T), region("R", T, 7 * T)
        scan_t = region("R", 192, 8 * T).rearrange("p (s r i) -> p s r i", s=3, r=2)
        scan_s = region("R", 1024, 8 * T + 192).rearrange("p (s r i n) -> p s r i n", s=2, r=2, i=PAIRS)
        cw = region("A", 10240).rearrange("p (k r i m) -> p k r i m", k=CHUNK + 1, r=2, i=PAIRS)
        lagk = region("A", 4096, 10240).rearrange("p (c j m) -> p c j m", c=8, j=CHUNK)
        bst = region("V", 2048).rearrange("p (r i m) -> p r i m", r=2, i=PAIRS)
        bt = [region("V", 1024, 2048 + 1024 * j).rearrange("p (i m) -> p i m", i=PAIRS) for j in range(2)]
        tail = at["A"] + 14336
        branch_n, branch_neg = view(tail, 512), view(tail + 512, 512)
        sc = [view(o, 512) for o in (tail + 1024, tail + 1536, tail + 4096, tail + 4608)]
        pt = view(tail + 2048, 2048).rearrange("p (a j n) -> p a j n", a=4, j=4)
        stat = region("stat", 64)
        vrows = region("W", 4096).rearrange("p (j n) -> p j n", j=4)
        kc = region("V", 4096).rearrange("p (s h n) -> p s h n", s=2, h=NH)
        vc = region("A", 16384).rearrange("p (b f n) -> p b f n", b=NS, f=2)
        soff = at["A"] + 16384
        smp_key = view(soff, 128)
        smp_soft = view(soff + 128, 257)
        smp_mult = view(soff + 400, 257)
        smp_pt = view(soff + 660, 128)
        smp_diag = view(soff + 790, 64)
        smp_new = view(soff + 860, 64)
        glu_t = view(soff + 924, 2 * T).rearrange("p (s n) -> p s n", s=2)
        glu_q = view(soff + 1964, 2 * T).rearrange("p (s n) -> p s n", s=2)
        z2 = k
        rz, ro = view(soff + 3004, T), region("rstd", T)
        x2 = xg
        ms = at["R"]
        x2row = view(ms, 4 * DM).rearrange("p (i n) -> p i n", i=4)
        x2_of = [x2row[:, i, :] for i in range(4)] + [region("V", DM, 512)]
        rowjunk = region("V", 512)
        ro_at = at["cos"]
        xrow = [view(ms + DM * j, DM) for j in range(2)]
        xtr = view(ms + 4096, 1536).rearrange("p (k n) -> p k n", k=16)
        sil = view(ms + 5632, 384)
        actt = view(ms + 6016, 384).rearrange("p (m n) -> p m n", m=4)
        yrow = view(ms + 6400, DM)
        slots = [at["R"] + 9424 + 8192 * j for j in range(4)] + [at["A"]]
        wg = [view(slots[0], 8192).rearrange("p (k n) -> p k n", k=16),
              view(slots[3], 8192).rearrange("p (k n) -> p k n", k=16)]
        wu = [view(slots[1], 8192).rearrange("p (k n) -> p k n", k=16),
              view(slots[4], 8192).rearrange("p (k n) -> p k n", k=16)]
        wd = view(slots[2], 8192).rearrange("p (k n) -> p k n", k=4)

        s_x = [sem(f"x_loaded{c}") for c in range(4)]
        s_const = sem("const_loaded")
        s_gc = sem("gains_loaded")
        s_par = sem("params_loaded")
        s_braw = sem("b_loaded")
        s_set = sem("constants_set")
        s_w = [sem(f"w_loaded{j}") for j in range(2)]
        s_sq = sem("squares_ready")
        s_xg = [sem(f"xg_ready{j}") for j in range(2)]
        s_part = sem("first_tile_parts")
        s_acc = sem("squares_added")
        s_ss = sem("sumsq_ready")
        s_root = sem("root_ready")
        s_rstd = sem("rstd_ready")
        s_proj = sem("proj_ready")
        s_uev = sem("u_ready")
        s_qev = sem("qkv_evacuated")
        s_rope = sem("qkv_ready")
        s_dve = sem("dve_chain")
        s_pool = sem("pool_chain")
        s_act = sem("act_chain")
        s_lact = sem("lambda_act")
        s_ldve = sem("lambda_dve")
        s_bw = sem("inject_weights_ready")
        s_inj = sem("inject_ready")
        s_injev = sem("inject_evacuated")
        s_scan = sem("scan_steps")
        s_state = sem("states_ready")
        s_out = sem("outputs_stored")
        s_kout, s_vout = sem("k_stored"), sem("v_stored")
        s_c = sem("c_loaded")
        s_cw = sem("c_weights_ready")
        s_vr, s_vrev = sem("v_transposed"), sem("v_rows_ready")
        s_attc = sem("attention_const_loaded")
        s_sco, s_msk, s_mx, s_exp = sem("scores_ready"), sem("scores_masked"), sem("max_ready"), sem("exp_ready")
        s_p, s_pt, s_ptev = sem("probs_ready"), sem("probs_transposed"), sem("probs_t_ready")
        s_o, s_oev = sem("o_ready"), sem("o_evacuated")
        s_samp = sem("sample_operands_ready")
        s_lag, s_lagc, s_lagd = sem("lag_psum_ready"), sem("lag_copied"), sem("lag_ready")
        s_y, s_z = sem("y_ready"), sem("z_ready")
        s_kc = [sem(f"cache_k{j}") for j in range(2)]
        s_vc = [sem(f"cache_v{j}") for j in range(NS)]
        s_gw = [sem(f"w_glu_loaded{j}") for j in range(4)]
        s_skey, s_skev = sem("sample_scores"), sem("sample_scores_copied")
        s_ssm, s_sexp, s_spr = sem("sample_scores_t"), sem("sample_exp"), sem("sample_probs")
        s_stp, s_stpc, s_spv, s_so = sem("sample_probs_t"), sem("sample_probs_t_copied"), sem("sample_pv"), sem("sample_o")
        s_smx = sem("sample_max")
        s_glu, s_sig, s_z2 = sem("glu_ready"), sem("sigmoid_ready"), sem("z2_ready")
        s_zsq, s_osq = sem("z_squares"), sem("o_squares")
        s_zss, s_oss = sem("z_sumsq"), sem("o_sumsq")
        s_zrt, s_ort = sem("z_root"), sem("o_root")
        s_mix = sem("mix_ready")
        s_x2l = sem("x_reloaded")
        s_op, s_x2 = sem("outproj_ready"), sem("x2_ready")
        s_rc = sem("router_const_loaded")
        s_gwr = sem("router_weights_ready")
        s_tr, s_trev = sem("x2_transposed"), sem("x2_rows_ready")
        s_rss, s_rrt, s_rrs = sem("row_sumsq"), sem("row_root"), sem("row_rstd")
        s_hr = sem("h_row_ready")
        s_x2st, s_hst = sem("x2_stored"), sem("h_stored")
        s_lg = sem("logits_psum")
        s_ml = sem("logits_zeroed")
        s_ra, s_rb = sem("router_act"), sem("router_dve")
        s_pos, s_posc = sem("positions_psum"), sem("positions_copied")
        s_sel, s_lst, s_idx = sem("selection_ready"), sem("lists_psum"), sem("indices_ready")
        s_e = {n: [sem(f"{n}_loaded{j}") for j in range(c)] for n, c in (("g", 2), ("u", 2), ("d", 1))}
        s_ig, s_is = sem("gather_index_ready"), sem("scatter_index_ready")
        s_gat, s_sct = [sem(f"rows_gathered{j}") for j in range(2)], sem("rows_scattered")
        s_xt, s_xte = sem("x_transposed"), sem("x_t_ready")
        s_ga, s_up, s_si, s_ac = sem("gate_psum"), sem("up_psum"), sem("silu_ready"), sem("act_ready")
        s_dn, s_yv = sem("down_psum"), sem("y_ready_rows")
        s_z0 = sem("rows_zeroed")
        s_fin, s_fq, s_fr, s_fo = sem("final_loaded"), sem("final_sumsq"), sem("final_root"), sem("final_ready")
        s_fst = sem("final_stored")
        s_finl = [sem(f"final_loaded{j}") for j in range(5)]
        s_held = sem("pool_waited")
        s_gf = sem("g_final_loaded")
        s_gt = sem("g_ffn_table_loaded")

        class Cols:
            def __init__(self, base):
                self.at = base

            def __call__(self, n):
                self.at += n
                return view(self.at - n, n)

        col = Cols(ro_at)
        row_part = col(20).rearrange("p (i g) -> p i g", g=4)
        row_sum, row_rstd = col(5), col(5)
        wr = col(576).rearrange("p (k n) -> p k n", k=16)
        rbias = col(36)
        iota_b, iota_s, valid, tok = col(NBLK), col(CAP), col(5), col(5)
        router_const = view(ro_at + 642, NBLK + CAP + 10)
        logit = col(180).rearrange("p (t n) -> p t n", t=5)
        keep = Cols(ms + 6400 + DM)
        gate_w = keep(10).rearrange("p (t j) -> p t j", t=5)
        idx_g = keep(NBLK + 2).bitcast(U32)
        idx_s = keep(NBLK + 1).bitcast(U32)
        idx_now = keep(4).bitcast(U32)
        none = keep(2 * LISTG)
        gtab = keep(16)
        ovexp = keep(NOV)
        ovexp_i = keep(NOV + 1).bitcast(U32)
        posblk = keep(5 * NBLK).rearrange("p (t b) -> p t b", t=5)
        rv16 = keep(5 * NBLK).bitcast(F16).rearrange("p (t b c) -> p t b c", t=5, c=2)
        upper16 = keep(64).bitcast(F16)
        ones16 = keep(64).bitcast(F16)
        m16 = keep(80).bitcast(F16).rearrange("p (t e) -> p t e", t=5)
        assert keep.at <= ms + 9424, keep.at - ms
        rt = Cols(at["A"])
        sel16 = [c.bitcast(F16).rearrange("p (t b s) -> p t b s", t=5, b=LISTG) for c in (yrow[:, 0:1680], rt(1680))]
        L32 = [rt(160).rearrange("p (t e) -> p t e", t=5) for _ in range(8)]
        B42 = [rt(5 * NBLK).rearrange("p (t b) -> p t b", t=5) for _ in range(5)]
        S5c = [rt(5) for _ in range(24)]
        E32 = [rt(32) for _ in range(8)]
        G20 = [rt(20).rearrange("p (t g) -> p t g", t=5) for _ in range(4)]
        ovt, ovt2 = (rt(NOV * NE).rearrange("p (o e) -> p o e", o=NOV) for _ in range(2))
        assert rt.at <= at["R"]
        assert col.at <= at["gmix"]

        glu_w = region("W", 4096).rearrange("p (s n) -> p s n", s=4)
        ujc = u[:, :, 0:SEQ].rearrange("p t (j c) -> p t j c", j=CHUNK)
        yjc = [ps[:, 2 * b, :].rearrange("p (j c) -> p j c", j=CHUNK) for b in range(2)]
        fx = [view(slots[0] + 6144 * b, DM) for b in range(5)]
        fy = [view(slots[0] + 6144 * b + DM, 2 * DM).rearrange("p (j n) -> p j n", j=2) for b in range(5)]
        fjunk, fg = view(slots[4], DM), view(slots[4] + DM, DM)
        fstat = stat[:, 0:10].rearrange("p (s n) -> p s n", s=2)
        TOKS = [P, P, P, P, NS]

        def pair(n):
            return ps[:, 2 * (n % 2):2 * (n % 2) + 2, 0:HALF]

        def halves(ap):
            return ap.rearrange("p (h n) -> p h n", h=2)

        def wide(ap, shape):
            return ap.to_broadcast(shape)

        def overflow_blocks(eng):
            eng.wait_ge(s_idx, NBLK // LISTG)
            return eng.value_load(ovexp_i[0:1, NOV:NOV + 1], min_val=0, max_val=NOV)

        def first(n):
            return type(n) is int and n == 0

        def blocks(eng, body):
            for j in range(2):
                body(j, j, 0)
            with eng.Fori(1, NE // 2) as it:
                for j in range(2):
                    body(it * 2 + j, j, it)
            more = overflow_blocks(eng)
            with eng.Fori(NE // 2, NBLK // 2) as it:
                for j in range(2):
                    with eng.If(it * 2 + (j - NE) < more):
                        body(it * 2 + j, j, it)
            return more

        block = ctx.enter_context(nc.Block())

        @block.sync
        def _(sp):
            def load_w(n, src):
                sp.dma_start(wring[:, n % 2].rearrange("p k n -> p (k n)"), src).then_inc(s_w[n % 2], 16)

            for c in range(4):
                sp.dma_start(xg[:, 4 * c:4 * c + 4, :], t["x_cols"][:, 4 * c:4 * c + 4, :]).then_inc(s_x[c], 16)
                if c == 0:
                    sp.dma_start(region("gmix", 56), t["g_cols"]).then_inc(s_gc, 16)
                    load_w(0, t["w_in"][0])
                if c == 1:
                    sp.dma_start(view(0, 2 * P), t["c_mats"]).then_inc(s_const, 16)
            load_w(1, t["w_in"][1])
            sp.dma_start(par, t["ssm_par"]).then_inc(s_par, 16)
            sp.dma_start(x0s, t["ssm_x0"]).then_inc(s_c, 16)
            sp.dma_start(view(at["cos"], 2 * T), t["c_rope"]).then_inc(s_rc, 16)
            sp.dma_start(braw, t["ssm_b_chan"]).then_inc(s_braw, 16)
            for n in range(2, 4):
                sp.wait_ge(s_proj, n - 1)
                load_w(n, t["w_in"][n])
            def load_tiles(a, b):
                with sp.Fori(a, b) as it:
                    for j in range(2):
                        sp.wait_ge(s_proj, it * 2 + (j - 1))
                        sp.dma_start(wring[:, j].rearrange("p k n -> p (k n)"),
                                     t["w_in"][bass.ds(it * 2 + j, 1)].rearrange("o p n -> (o p) n")
                                     ).then_inc(s_w[j], 16)

            load_tiles(2, 8)
            sp.wait_ge(s_bw, 1)
            sp.wait_ge(s_ldve, 4)
            sp.dma_start(view(tail, 1024), t["c_branch"]).then_inc(s_attc, 16)
            load_tiles(8, 16)
            sp.wait_ge(s_rope, 16)
            sp.dma_start(t["k_out"], k).then_inc(s_kout, 16)
            sp.wait_ge(s_rope, 24)
            sp.dma_start(t["v_out"], v).then_inc(s_vout, 16)
            sp.dma_start(view(ro_at + 30, 576), t["w_router"]).then_inc(s_rc, 16)
            sp.dma_start(rbias, t["b_router"].to_broadcast([P, 36])).then_inc(s_rc, 16)
            sp.dma_start(router_const, t["c_router"]).then_inc(s_rc, 16)
            sp.dma_start(region("upper", P), t["c_upper"]).then_inc(s_rc, 16)
            sp.wait_ge(s_proj, 32)
            sp.wait_ge(s_state, 1)
            sp.dma_start(cw[:, 0], t["ssm_c"]).then_inc(s_c, 16)
            sp.wait_ge(s_vout, 16)
            sp.wait_ge(s_vr, 8)
            sp.wait_ge(s_samp, 2)
            sp.dma_start(bst, t["ssm_b_state"]).then_inc(s_c, 16)
            with nc.allow_non_contiguous_dma(reason="one column per state"):
                for r in range(2):
                    sp.dma_start(t["state_out"][:, r, :, 0:1], xs[:, r, :, NCH:NCH + 1]).then_inc(s_out, 16)
                    sp.dma_start(t["state_out"][:, r, :, 1:9], xns[:, r]).then_inc(s_out, 16)
            sp.wait_ge(s_lag, 1)

            def load_keys(b):
                sp.dma_start(kc[:, b % 2].rearrange("p h n -> p (h n)"), t["k_cache"][b]).then_inc(s_kc[b % 2], 16)

            for b in range(2):
                load_keys(b)
            sp.wait_ge(s_o, NH)
            sp.dma_start(smp_mult[0:64, :], t["c_sample"]).then_inc(s_attc, 16)
            for n in range(4):
                sp.dma_start(glu_w[:, n], t["w_glu"][n]).then_inc(s_gw[n], 16)
            for b in range(2, NS):
                sp.wait_ge(s_skey, b - 1)
                load_keys(b)
            sp.wait_ge(s_y, 8)
            for b in range(NS):
                sp.dma_start(vc[:, b].rearrange("p f n -> p (f n)"), t["v_cache"][b]).then_inc(s_vc[b], 16)
            for n in range(4, 8):
                sp.wait_ge(s_glu, n - 3)
                sp.dma_start(glu_w[:, n % 4], t["w_glu"][n]).then_inc(s_gw[n % 4], 16)
            for n in range(2):
                sp.wait_ge(s_glu, 6 + 2 * n)
                load_w(n, t["w_out"][n])
            sp.wait_ge(s_spv, NS)
            sp.dma_start(x2, t["x_cols"]).then_inc(s_x2l, 16)

            def store_x2(g):
                c = slice(512 * g, 512 * (g + 1))
                sp.wait_ge(s_trev, 5 * (g + 1))
                sp.dma_start(x2_rows[0:SEQ, c].rearrange("(i p) n -> p i n", p=P), x2row[:, 0:4, c]
                             ).then_inc(s_x2st, 16)
                sp.dma_start(x2_rows[SEQ:T, c], x2_of[4][0:NS, c]).then_inc(s_x2st, 16)

            for n in range(2, 16):
                if n % 4 == 3 and n > 4:
                    store_x2(n // 4 - 1)
                sp.wait_ge(s_op, n - 1)
                load_w(n, t["w_out"][n])
            store_x2(3)

            def gate(e, j):
                sp.dma_start(wg[j], t["w_gate"][bass.ds(e, 1)].rearrange("o (p k) n -> (o p) k n", k=16)
                             ).then_inc(s_e["g"][j], 16)

            def up(e, j):
                sp.dma_start(wu[j], t["w_up"][bass.ds(e, 1)].rearrange("o (p k) n -> (o p) k n", k=16)
                             ).then_inc(s_e["u"][j], 16)

            def down(e):
                sp.dma_start(wd, t["w_down"][bass.ds(e, 1)].rearrange("o (k p) n -> p (o k) n", k=4)
                             ).then_inc(s_e["d"][0], 16)

            sp.wait_ge(s_op, 16)
            gate(0, 0)
            for i, n in enumerate(TOKS):
                sp.wait_ge(s_hr, i + 1)
                sp.dma_start(h_rows[P * i:P * i + n, :], x2_of[i][0:n]).then_inc(s_hst, 16)
            sp.dma_start(gtab, t["g_ffn"].rearrange("o (p k) -> (o p) k", k=16)).then_inc(s_gt, 16)
            sp.wait_ge(s_hst, 16 * 5)
            up(0, 0)
            down(0)
            for j in range(2):
                sp.wait_ge(s_gat[j], 16)
            gate(1, 1)
            sp.wait_ge(s_lst, NBLK // LISTG)
            up(1, 1)

            def loads(m, j):
                sp.wait_ge(s_ga, m + 1)
                gate(m + 2, j)
                sp.wait_ge(s_up, m + 1)
                up(m + 2, j)
                sp.wait_ge(s_dn, m * 4 + 4)
                down(m + 1)

            with sp.Fori(0, NE // 2 - 1) as it:
                for j in range(2):
                    loads(it * 2 + j, j)
            sp.wait_ge(s_dn, 4 * (NE - 1))
            down(NE - 1)
            more = overflow_blocks(sp)
            with sp.Fori(NE // 2, NBLK // 2) as it:
                for j in range(2):
                    with sp.If(it * 2 + (j - NE) < more):
                        e = sp.value_load(ovexp_i[0:1, bass.ds(it * 2 + (j - NE), 1)], min_val=0, max_val=NE - 1)
                        sp.wait_ge(s_ga, it * 2 + (j - 1))
                        gate(e, j)
                        sp.wait_ge(s_up, it * 2 + (j - 1))
                        up(e, j)
                        sp.wait_ge(s_dn, it * 8 + 4 * j)
                        down(e)
            sp.wait_ge(s_dn, more * 4 + 4 * NE)
            sp.wait_ge(s_x2st, 16 * 8)
            sp.dma_start(fg, t["g_final"].to_broadcast([P, DM])).then_inc(s_gf, 16)
            for i, n in enumerate(TOKS):
                sp.dma_start(fx[i][0:n], x2_rows[P * i:P * i + n, :]).then_inc(s_finl[i], 16)
            sp.wait_ge(s_sct, more * 16 + 16 * NE)
            for i, n in enumerate(TOKS):
                sp.dma_start(fy[i][0:n].rearrange("p j n -> p (j n)"),
                             y_rows[2 * P * i:2 * P * i + 2 * n, :].rearrange("(p j) n -> p (j n)", j=2)
                             ).then_inc(s_finl[i], 16)
            for i, n in enumerate(TOKS):
                sp.wait_ge(s_fo, i + 1)
                sp.dma_start(t["y_out"][P * i:P * i + n, :], fx[i][0:n]).then_inc(s_fst, 16)
            sp.wait_ge(s_fst, 16 * 5)
            sp.wait_ge(s_out, 16 * 4)
            sp.wait_ge(s_kout, 16)
            sp.wait_ge(s_vout, 16)
            sp.wait_ge(s_hst, 16 * 5)

        @block.tensor
        def _(pe):
            mm = pe.matmul
            def product(n, w, rhs, k0, kn, stop=True):
                for kk in range(k0, kn):
                    for h in range(2):
                        last = mm(pair(n)[:, h, :], w(kk), rhs(kk)[:, HALF * h:HALF * (h + 1)],
                                  start=(kk == 0), stop=(kk == kn - 1 and stop))
                return last

            def proj(j, count, freed):
                pe.wait_ge(s_w[j], count)
                if freed is not None:
                    pe.wait_ge(*freed)
                product(j, lambda kk: wring[:, j, kk, :], lambda kk: xg[:, kk, :], 0, 16).then_inc(s_proj, 1)

            pe.wait_ge(s_w[0], 16)
            for c in range(4):
                pe.wait_ge(s_xg[c % 2], c // 2 + 1)
                product(0, lambda kk: wring[:, 0, kk, :], lambda kk: xg[:, kk, :], 4 * c, 4 * c + 4, stop=(c == 3)
                        ).then_inc(s_proj if c == 3 else s_part, 1)
            pe.wait_ge(s_const, 16)
            pe.wait_ge(s_acc, 4)
            for h in range(2):
                last = mm(ps[:, 4 + h, 0:HALF], ones, sq[:, 0, 0, HALF * h:HALF * (h + 1)], start=True, stop=True)
            last.then_inc(s_ss, 1)
            for n in range(1, 8):
                proj(n % 2, 16 * (n // 2 + 1), (s_uev, 3 * (n - 1)) if n >= 2 else None)
            pe.wait_ge(s_bw, 1)
            pe.wait_ge(s_uev, 24)
            pe.wait_ge(s_root, 1)
            for n in range(4):
                ri, c0, bank = n // 2, 4 * (n % 2), 4 * (1 - n % 2)
                if n >= 2:
                    pe.wait_ge(s_injev, 4 * (n - 1))
                for ct in range(4):
                    for j in range(CHUNK):
                        for r in range(4):
                            last = mm(ps[:, bank + r, P * ct:P * (ct + 1)],
                                      bw[32 * r:32 * r + 32, CHUNK - 1 - j, ri, c0 + ct, :],
                                      ujc[32 * r:32 * r + 32, c0 + ct, j, :], start=(j == 0), stop=(j == CHUNK - 1))
                            if ct == 3 and j == CHUNK - 1:
                                last.then_inc(s_inj, 1)
            pe.wait_ge(s_injev, 12)
            for n in range(16):
                for r in range(4):
                    last = mm(ps[:, 4 + r, NS * n:NS * (n + 1)], bw[32 * r:32 * r + 32, 0, n // 8, n % 8, :],
                              u[32 * r:32 * r + 32, n % 8, SEQ:T], start=True, stop=True)
                    if n == 15:
                        last.then_inc(s_inj, 1)
            pe.wait_ge(s_injev, 16)
            for n in (8, 9):
                proj(n % 2, 16 * (n // 2 + 1), (s_uev, 24))
            with pe.Fori(5, 16) as it:
                for j in range(2):
                    proj(j, it * 16 + 16, (s_qev, it * 2 + (j - 9)))
            pe.wait_ge(s_rope, 24)
            pe.wait_ge(s_injev, 20)
            for n in range(8):
                j, hh = n // 2, n % 2
                if n >= 4:
                    pe.wait_ge(s_vrev, n - 3)
                for h in range(4):
                    last = pe.transpose(ps[:, 4 + n % 4, P * h:P * (h + 1)],
                                        v[:, 4 * hh + h, P * j:P * (j + 1)], ident)
                last.then_inc(s_vr, 1)

            def scores(a):
                h, qt = a // 4, a % 4
                if a >= 4:
                    pe.wait_ge(s_msk, a - 3)
                mm(ps[:, qt, 0:P * (qt + 1)], q[:, h, P * qt:P * (qt + 1)], k[:, h, 0:P * (qt + 1)],
                   start=True, stop=True).then_inc(s_sco, 1)

            def turn(a):
                pe.wait_ge(s_p, a + 1)
                if a >= 2:
                    pe.wait_ge(s_ptev, a - 1)
                for j in range(a % 4 + 1):
                    last = pe.transpose(ps[:, 4 + a % 2, P * j:P * (j + 1)], sc[a % 4][:, P * j:P * (j + 1)], ident)
                last.then_inc(s_pt, 1)

            def weigh(h):
                pe.wait_ge(s_ptev, 4 * h + 4)
                if h >= 2:
                    pe.wait_ge(s_oev, h - 1)
                for j in range(4):
                    last = mm(ps[:, 6 + h % 2, P * j:SEQ].rearrange("p (a n) -> p a n", n=P),
                              vrows[:, j, P * h:P * (h + 1)], pt[:, j:4, j, :], start=(j == 0), stop=(j == 3))
                last.then_inc(s_o, 1)

            pe.wait_ge(s_qev, 24)
            for a in range(4):
                scores(a)
            pe.wait_ge(s_vrev, 8)
            for a in range(4 * NH):
                if a + 4 < 4 * NH:
                    scores(a + 4)
                turn(a)
                if a % 4 == 3:
                    weigh(a // 4)
            pe.wait_ge(s_cw, 1)
            pe.wait_ge(s_msk, 4 * NH)
            for i in range(PAIRS):
                r, ct = i % 4, i // 4
                for ri in range(2):
                    last = mm(ps[32 * r:32 * r + 32, ct // 4, P * (ct % 4):P * (ct % 4 + 1)].rearrange(
                        "p (j m) -> p j m", j=CHUNK), bst[:, ri, i, :], cw[:, 0:CHUNK, ri, i, :],
                        start=(ri == 0), stop=(ri == 1))
            last.then_inc(s_lag, 1)
            pe.wait_ge(s_lagd, 1)
            pe.wait_ge(s_state, 1)
            for ct in range(8):
                b = ct % 2
                if ct >= 2:
                    pe.wait_ge(s_z, ct - 1)
                for lag in range(CHUNK):
                    mm(yjc[b][:, lag:CHUNK, :], lagk[:, ct, lag, :], ujc[:, ct, 0:CHUNK - lag, :],
                       start=(lag == 0), stop=False, skip_group_check=True)
                for r in range(4):
                    i = 4 * ct + r
                    for j in range(CHUNK):
                        for ri in range(2):
                            mm(yjc[b][32 * r:32 * r + 32, j, :], cw[:, j + 1, ri, i, :], xs[:, ri, i, 0:NCH],
                               start=False, stop=(j == CHUNK - 1 and ri == 1), skip_group_check=True)
                ys = ps[:, 2 * b + 1, 0:NS]
                mm(ys, lagk[:, ct, 0, :], u[:, ct, SEQ:T], start=True, stop=False, skip_group_check=True)
                for r in range(4):
                    i = 4 * ct + r
                    for ri in range(2):
                        last = mm(ys[32 * r:32 * r + 32, :], cw[:, 1, ri, i, :], x0s[:, ri, i, :],
                                  start=False, stop=(ri == 1), skip_group_check=True)
                last.then_inc(s_y, 1)
                if ct == 0:
                    pe.wait_ge(s_oev, NH)
                pe.wait_ge(s_kc[ct % 2], 16 * (ct // 2 + 1))
                for h in range(NH):
                    for f in range(2):
                        c = 64 * f + 8 * ct + h
                        last = mm(ps[:, 6, c:c + 1], kc[:, ct % 2, h, P * f:P * (f + 1)],
                                  q[:, h, SEQ + ct:SEQ + ct + 1], start=True, stop=True)
                last.then_inc(s_skey, 1)
            pe.wait_ge(s_z, 8)
            pe.wait_ge(s_ptev, 4 * NH)

            def sum_sq(n, squares, done, banks):
                pe.wait_ge(squares, n + 1)
                for h in range(2):
                    last = mm(ps[:, banks + h, 0:HALF], ones, glu_q[:, n % 2, HALF * h:HALF * (h + 1)],
                              start=(n == 0), stop=(n == 7))
                last.then_inc(done, 1)

            def turn_scores():
                pe.wait_ge(s_skev, 1)
                for f in range(2):
                    pe.transpose(ps[0:64, 7, P * f:P * (f + 1)], smp_key[:, 64 * f:64 * (f + 1)], ident)
                mm(ps[0:64, 7, 2 * P:2 * P + 1], prod, ones[:, 0:1], start=True, stop=True).then_inc(s_ssm, 1)

            def turn_probs():
                pe.wait_ge(s_spr, 1)
                for f in range(2):
                    pe.transpose(ps[:, 6, 64 * f:64 * (f + 1)], smp_soft[0:64, P * f:P * (f + 1)], ident[0:64, 0:64])
                mm(ps[:, 6, P:P + 64], ones[0:64, :], smp_diag[0:64, :], start=True, stop=True).then_inc(s_stp, 1)

            def weigh_sample(b):
                if b == 0:
                    pe.wait_ge(s_stpc, 1)
                pe.wait_ge(s_vc[b], 16)
                for h in range(NH):
                    for f in range(2):
                        c = 8 * b + h
                        last = mm(ps[:, 7, c:c + 1], vc[:, b, f, P * h:P * (h + 1)],
                                  smp_pt[:, 64 * f + c:64 * f + c + 1], start=(f == 0), stop=(f == 1))
                last.then_inc(s_spv, 1)

            for n in range(8):
                pe.wait_ge(s_gw[n % 4], 16 * (n // 4 + 1))
                if n >= 2:
                    pe.wait_ge(s_sig, n - 1)
                gw = glu_w[:, n % 4].rearrange("p (k m) -> p k m", k=8)
                product(n, lambda kk: gw[:, kk, :], lambda kk: u[:, kk, :], 0, 8).then_inc(s_glu, 1)
                if n == 0:
                    turn_scores()
                if n >= 2:
                    sum_sq(n - 2, s_zsq, s_zss, 4)
                if n == 2:
                    turn_probs()
                if 3 <= n < 7:
                    weigh_sample(2 * (n - 3))
                    weigh_sample(2 * (n - 3) + 1)
            sum_sq(6, s_zsq, s_zss, 4)
            sum_sq(7, s_zsq, s_zss, 4)

            def rows_of_x2(g):
                pe.wait_ge(s_x2, 4 * g + 4)
                if g == 0:
                    pe.wait_ge(s_gwr, 1)
                for i, n in enumerate(TOKS):
                    b = 5 * g + i
                    if b >= 3:
                        pe.wait_ge(s_trev, b - 2)
                    for m in range(4):
                        last = pe.transpose(ps[0:n, 4 + b % 3, P * m:P * (m + 1)],
                                            x2[:, 4 * g + m, P * i:P * i + n], ident)
                    last.then_inc(s_tr, 1)
                for i, n in enumerate(TOKS):
                    for kk in range(4 * g, 4 * g + 4):
                        last = mm(ps[0:n, 7, 36 * i:36 * (i + 1)], x2[:, kk, P * i:P * i + n], wr[:, kk, :],
                                  start=(kk == 0 and i == 0), stop=(kk == 15), skip_group_check=True)
                if g == 3:
                    last.then_inc(s_lg, 1)

            def outproj(n, k0, kn):
                for kk in range(k0, kn):
                    if n == 0:
                        pe.wait_ge(s_mix, kk + 1)
                    last = product(n, lambda kk: wring[:, n % 2, kk, :],
                                   lambda kk: z2[:, kk, :] if kk < 8 else q[:, kk - 8, :], kk, kk + 1, stop=(kk == 15))
                return last

            pe.wait_ge(s_sig, 8)
            for n in range(2):
                pe.wait_ge(s_w[n % 2], 16 * 17)
                outproj(n, 0, 8)
                if n == 0:
                    pe.wait_ge(s_so, 1)
                for m in range(4 * n, 4 * n + 4):
                    sum_sq(m, s_osq, s_oss, 6)
            for n in range(16):
                if n >= 2:
                    pe.wait_ge(s_w[n % 2], 16 * (16 + n // 2 + 1))
                    pe.wait_ge(s_x2, n - 1)
                outproj(n, 8 if n < 2 else 0, 16).then_inc(s_op, 1)
                if n % 4 == 0 and n:
                    rows_of_x2(n // 4 - 1)
            rows_of_x2(3)
            pe.wait_ge(s_rb, 1)
            for i in range(6):
                for ii in range(min(i, 4) + 1):
                    last = mm(ps[:, 1, 32 * i:32 * (i + 1)], upper16 if ii == i else ones16, m16[:, ii, :],
                              start=(ii == 0), stop=(ii == min(i, 4)))
            last.then_inc(s_pos, 1)
            pe.wait_ge(s_trev, 20)

            def lists(g):
                pe.wait_ge(s_sel, g + 1)
                if g >= 2:
                    pe.wait_ge(s_idx, g - 1)
                for b in range(LISTG):
                    for i in range(5):
                        last = mm(ps[0:CAP, 4 + g % 2, 2 * b:2 * b + 2], sel16[g % 2][:, i, b, :],
                                  rv16[:, i, LISTG * g + b, :], start=(i == 0), stop=(i == 4))
                last.then_inc(s_lst, 1)

            def turn_rows(n, j, it):
                pe.wait_ge(s_gat[j], it * 16 + 16)
                rows = xrow[j][0:CAP, :].rearrange("p (m k) -> p k m", k=16)
                for g in range(4):
                    if not first(n) or g >= 2:
                        pe.wait_ge(s_xte, n * 4 + (g - 1))
                    for m in range(5 * g, min(5 * g + 5, 16)):
                        last = pe.transpose(ps[:, g % 2, CAP * (m - 5 * g):CAP * (m - 5 * g + 1)], rows[:, m, :],
                                            ident[0:CAP, 0:CAP])
                    last.then_inc(s_xt, 1)

            def expert(n, j, it):
                pe.wait_ge(s_e["g"][j], it * 16 + 16)
                pe.wait_ge(s_xte, n * 4 + 4)
                for m in range(4):
                    for kk in range(16):
                        last = mm(ps[:, 2, CAP * m:CAP * (m + 1)], wg[j][:, kk, P * m:P * (m + 1)],
                                  xtr[:, kk, :], start=(kk == 0), stop=(kk == 15))
                last.then_inc(s_ga, 1)
                if first(n):
                    for g in range(3, NBLK // LISTG):
                        lists(g)
                pe.wait_ge(s_e["u"][j], it * 16 + 16)
                for m in range(4):
                    for kk in range(16):
                        last = mm(ps[:, 3, CAP * m:CAP * (m + 1)], wu[j][:, kk, P * m:P * (m + 1)],
                                  xtr[:, kk, :], start=(kk == 0), stop=(kk == 15))
                last.then_inc(s_up, 1)
                turn_rows(n + 1, 1 - j, it + j)
                pe.wait_ge(s_e["d"][0], n * 16 + 16)
                pe.wait_ge(s_ac, n + 1)
                if first(n):
                    pe.wait_ge(s_idx, NBLK // LISTG)
                else:
                    pe.wait_ge(s_yv, n * 4)
                for c in range(4):
                    for kk in range(4):
                        last = mm(ps[0:CAP, 4 + c, :], actt[:, kk, :], wd[:, kk, 512 * c:512 * (c + 1)],
                                  start=(kk == 0), stop=(kk == 3))
                    last.then_inc(s_dn, 1)

            for g in range(3):
                lists(g)
            turn_rows(0, 0, 0)
            blocks(pe, expert)

        @block.scalar
        def _(act):
            A = act.activation
            for c in range(4):
                act.wait_ge(s_x[c], 16)
                if c >= 2:
                    act.wait_ge(s_acc, c - 1)
                A(sq[:, min(c, 1)], xg[:, 4 * c:4 * c + 4, :], ACT.Square).then_inc(s_sq, 1)
                if c % 2 == 0:
                    act.wait_ge(s_gc, 16)
                    act.wait_ge(s_sq, c + 1)
                    for kk in range(4 * c, 4 * c + 4):
                        last = A(xg[:, kk, :], xg[:, kk, :], ACT.Copy, scale=gmix[:, kk:kk + 1])
                    last.then_inc(s_xg[0], 1)
            act.wait_ge(s_set, 1)
            act.wait_ge(s_par, 16)
            A(par[:, 2, :], par[:, 2, :], ACT.Exp).then_inc(s_lact, 1)
            act.wait_ge(s_ldve, 1)
            A(tmp[2], tmp[0], ACT.Exp).then_inc(s_lact, 1)
            act.wait_ge(s_ss, 1)
            A(halves(rstd), ps[:, 4:6, 0:HALF], ACT.Sqrt, bias=eps, scale=1.0 / DM).then_inc(s_root, 1)
            act.wait_ge(s_ldve, 2)
            A(tmp[5], tmp[4], ACT.Sin).then_inc(s_lact, 1)
            A(tmp[6], tmp[4], ACT.Sin, scale=0.5).then_inc(s_lact, 1)
            act.wait_ge(s_bw, 1)
            for n in range(4):
                ri, c0, bank = n // 2, 4 * (n % 2), 4 * (1 - n % 2)
                act.wait_ge(s_inj, 4 * (n + 1))
                for r in range(4):
                    A(xs[:, ri, 4 * c0 + r:4 * c0 + r + 13:4, 1:NCH + 1],
                      ps[:, bank + r, :].rearrange("p (c n) -> p c n", c=4), ACT.Copy).then_inc(s_injev, 1)
            act.wait_ge(s_inj, 20)
            for r in range(4):
                A(xns[:, :, r:r + 29:4, :], ps[:, 4 + r, 0:16 * NS].rearrange("p (r c n) -> p r c n", r=2, c=8),
                  ACT.Copy).then_inc(s_injev, 1)
            for m in range(24):
                act.wait_ge(s_proj, m + 9)
                if m >= 2:
                    act.wait_ge(s_rope, m - 1)
                if m == 0:
                    act.wait_ge(s_ldve, 4)
                    act.wait_ge(s_bw, 1)
                if m < 16:
                    A(halves(rope_in[0:64, m % 2, 1]), pair(m)[64:128], ACT.Copy)
                    A(halves(rope_in[64:128, m % 2, 1]), pair(m)[0:64], ACT.Copy)
                A(halves(rope_in[:, m % 2, 0]), pair(m), ACT.Copy).then_inc(s_qev, 1)
            for n in range(8):
                act.wait_ge(s_vr, n + 1)
                if n == 0:
                    act.wait_ge(s_proj, 32)
                A(vrows[:, n // 2, 512 * (n % 2):512 * (n % 2 + 1)], ps[:, 4 + n % 4, :], ACT.Copy).then_inc(s_vrev, 1)

            def exps(a):
                act.wait_ge(s_mx, a + 1)
                w = P * (a % 4 + 1)
                A(sc[a % 4][:, 0:w], sc[a % 4][:, 0:w], ACT.Exp, bias=stat[:, a:a + 1], scale=SCALE).then_inc(s_exp, 1)

            def turned(a):
                act.wait_ge(s_pt, a + 1)
                if a % 4 == 0 and a:
                    act.wait_ge(s_o, a // 4)
                qt = a % 4
                A(pt[:, qt, 0:qt + 1, :], ps[:, 4 + a % 2, 0:P * (qt + 1)].rearrange("p (j n) -> p j n", n=P),
                  ACT.Copy).then_inc(s_ptev, 1)

            def head_out(h):
                act.wait_ge(s_o, h + 1)
                A(q[:, h, 0:SEQ], ps[:, 6 + h % 2, :], ACT.Copy).then_inc(s_oev, 1)

            exps(0)
            for a in range(4 * NH):
                if a + 1 < 4 * NH:
                    exps(a + 1)
                turned(a)
                if a % 4 == 1 and a > 4:
                    head_out(a // 4 - 1)
            head_out(NH - 1)
            act.wait_ge(s_lag, 1)
            act.wait_ge(s_lagc, 1)
            for r in range(4):
                last = A(lagk[32 * r:32 * r + 32, :, :, 32 * r:32 * r + 32],
                         psum_t[32 * r:32 * r + 32, 0:1024].rearrange("p (c j m) -> p c j m", c=8, j=CHUNK), ACT.Copy)
            last.then_inc(s_lagc, 1)
            for ct in range(8):
                act.wait_ge(s_y, ct + 1)
                A(u[:, ct, 0:SEQ].rearrange("p (c j) -> p j c", j=CHUNK), yjc[ct % 2], ACT.Gelu_apprx_tanh)
                A(u[:, ct, SEQ:T], ps[:, 2 * (ct % 2) + 1, 0:NS], ACT.Gelu_apprx_tanh).then_inc(s_z, 1)

            def squares(n, src, ready, count, freed, freed_at, done):
                act.wait_ge(ready, count)
                if freed_at > 0:
                    act.wait_ge(freed, freed_at)
                A(glu_q[:, n % 2], src[:, n, :], ACT.Square).then_inc(done, 1)

            act.wait_ge(s_skey, NS)
            A(smp_key, ps[:, 6, 0:128], ACT.Copy).then_inc(s_skev, 1)
            for n in range(8):
                act.wait_ge(s_glu, n + 1)
                if n >= 2:
                    act.wait_ge(s_z2, n - 1)
                A(halves(glu_t[:, n % 2]), pair(n), ACT.Sigmoid).then_inc(s_sig, 1)
                if n == 0:
                    act.wait_ge(s_smx, 1)
                    A(smp_soft[0:64], smp_soft[0:64], ACT.Exp, bias=stat[0:64, 40:41], scale=SCALE).then_inc(s_sexp, 1)
                if n == 2:
                    act.wait_ge(s_stp, 1)
                    A(smp_pt, ps[:, 6, 0:128], ACT.Copy)
                    A(smp_new, ps[:, 6, P:P + 64], ACT.Copy).then_inc(s_stpc, 1)
                if n >= 1:
                    squares(n - 1, z2, s_z2, n, s_zss, n - 2, s_zsq)
            squares(7, z2, s_z2, 8, s_zss, 6, s_zsq)
            act.wait_ge(s_zss, 8)
            A(halves(rz), ps[:, 4:6, 0:HALF], ACT.Sqrt, bias=eps, scale=1.0 / (8 * P)).then_inc(s_zrt, 1)
            for n in range(8):
                squares(n, q, s_so, 1, s_oss, n - 1, s_osq)
            act.wait_ge(s_oss, 8)
            A(halves(ro), ps[:, 6:8, 0:HALF], ACT.Sqrt, bias=eps, scale=1.0 / (8 * P)).then_inc(s_ort, 1)
            for b in range(20):
                g, i = b // 5, b % 5
                n = TOKS[i]
                part = x2_of[i][0:n, 512 * g:512 * (g + 1)]
                act.wait_ge(s_tr, b + 1)
                A(part, ps[0:n, 4 + b % 3, :], ACT.Copy).then_inc(s_trev, 1)
                act.wait_ge(s_trev, b + 1)
                if b:
                    act.wait_ge(s_rss, b)
                A(rowjunk[0:n], part, ACT.Square, accum_out=row_part[0:n, i, g:g + 1]).then_inc(s_rss, 1)
            act.wait_ge(s_rrs, 1)
            A(row_sum, row_sum, ACT.Sqrt, bias=eps, scale=1.0 / DM).then_inc(s_rrt, 1)
            act.wait_ge(s_rrs, 2)
            act.wait_ge(s_x2st, 16 * 8)
            for i, n in enumerate(TOKS):
                A(x2_of[i][0:n], x2_of[i][0:n], ACT.Copy, scale=row_rstd[0:n, i:i + 1]).then_inc(s_hr, 1)
            act.wait_ge(s_ra, 1)
            A(G20[2], G20[2], ACT.Exp).then_inc(s_ra, 1)
            act.wait_ge(s_ra, 3)
            A(S5c[5], S5c[5], ACT.Exp).then_inc(s_ra, 1)

            def expert(n, j, it):
                act.wait_ge(s_ga, n + 1)
                if not first(n):
                    act.wait_ge(s_ac, n)
                A(sil, ps[:, 2, 0:4 * CAP], ACT.Silu).then_inc(s_si, 1)
                if not first(n):
                    act.wait_ge(s_sct, n * 16)
                for c in range(4):
                    act.wait_ge(s_dn, n * 4 + (c + 1))
                    A(yrow[0:CAP, 512 * c:512 * (c + 1)], ps[0:CAP, 4 + c, :], ACT.Copy).then_inc(s_yv, 1)

            more = blocks(act, expert)
            for i, n in enumerate(TOKS):
                act.wait_ge(s_fin, i + 1)
                A(fjunk[0:n], fx[i][0:n], ACT.Square, accum_out=fstat[0:n, 0, i:i + 1]).then_inc(s_fq, 1)
                act.wait_ge(s_fq, i + 1)
                A(fstat[0:n, 0, i:i + 1], fstat[0:n, 0, i:i + 1], ACT.Sqrt, bias=eps[0:n], scale=1.0 / DM
                  ).then_inc(s_fr, 1)

        @block.gpsimd
        def _(pool):
            chain = [0]

            def link(ins):
                chain[0] += 1
                ins.then_inc(s_pool, 1)
                pool.wait_ge(s_pool, chain[0])

            tt = pool.tensor_tensor

            def complex_product(outs, a, b, t, negated=False):
                (ar, ai), (br, bi), (tr, ti) = a, b, t
                s1, s2 = (ALU.add, ALU.subtract) if negated else (ALU.subtract, ALU.add)
                tt(tr, ar, br, ALU.mult)
                link(tt(ti, ai, bi, ALU.mult))
                link(tt(outs[0], tr, ti, s1))
                tt(tr, ai, br, ALU.mult)
                link(tt(ti, ar, bi, ALU.mult))
                link(tt(outs[1], tr, ti, s2))

            pool.wait_ge(s_ldve, 3)
            pool.wait_ge(s_braw, 16)
            flat = [[bw[:, kk, r].rearrange("p c n -> p (c n)") for r in range(2)] for kk in range(CHUNK)]
            two = (tmp[4][:, 0:1024], tmp[5][:, 0:1024])
            complex_product(flat[0], (braw[:, 0], braw[:, 1]), (cre[:, 0:1024], cim[:, 0:1024]), two)
            for kk in range(1, CHUNK):
                complex_product(flat[kk], flat[kk - 1], (lre[:, 0:1024], lim[:, 0:1024]), two)
            tt(two[0][:, 0:1], two[0][:, 0:1], two[0][:, 0:1], ALU.mult).then_inc(s_bw, 1)
            pool.wait_ge(s_rstd, 1)
            pool.wait_ge(s_rc, 16)
            pool.wait_ge(s_bw, 1)
            tt(cosr, cos, rstd, ALU.mult)
            link(tt(sinr, sin, rstd, ALU.mult))
            for m in range(24):
                pool.wait_ge(s_qev, m + 1)
                dst = (q, k, v)[m // 8][:, m % 8, :]
                if m < 16:
                    if m == 0:
                        pool.wait_ge(s_inj, 20)
                    tt(rope_t[:, 0], rope_in[:, m % 2, 0], cosr, ALU.mult)
                    link(tt(rope_t[:, 1], rope_in[:, m % 2, 1], sinr, ALU.mult))
                    tt(dst, rope_t[:, 0], rope_t[:, 1], ALU.add).then_inc(s_rope, 1)
                    pool.wait_ge(s_rope, m + 1)
                else:
                    tt(dst, rope_in[:, m % 2, 0], rstd, ALU.mult).then_inc(s_rope, 1)
            pool.wait_ge(s_proj, 32)
            pool.wait_ge(s_rope, 24)
            pool.wait_ge(s_state, 1)
            link(pool.memset(lagk, 0.0))
            pool.wait_ge(s_c, 16 * 3)
            link(pool.tensor_scalar(cw[:, 0, 1], cw[:, 0, 1], -1.0, None, ALU.mult))
            def over(ap):
                return ap.unsqueeze(2).to_broadcast([P, PAIRS, 32])
            lam = (over(lamp[:, 0]), over(lamp[:, 1]))
            for kk in range(1, CHUNK + 1):
                complex_product((cw[:, kk, 0], cw[:, kk, 1]), (cw[:, kk - 1, 0], cw[:, kk - 1, 1]), lam, bt, True)
            tr, ti = bt
            cr, ci = over(coef[:, 0]), over(coef[:, 1])
            tt(tr, bst[:, 0], cr, ALU.mult)
            link(tt(ti, bst[:, 1], ci, ALU.mult))
            link(tt(tr, tr, ti, ALU.subtract))
            link(tt(ti, bst[:, 0], ci, ALU.mult))
            link(pool.tensor_copy(bst[:, 0], tr))
            link(tt(tr, bst[:, 1], cr, ALU.mult))
            tt(bst[:, 1], tr, ti, ALU.add).then_inc(s_cw, 1)
            pool.wait_ge(s_cw, 1)
            pool.memset(stat[:, 63:64], 0.0).then_inc(s_lagc, 1)

            def held():
                pool.sem_inc(s_held, 1)

            def gather(n, j):
                pool.wait_ge(s_ig, n + 1)
                held()
                pool.indirect_dma_start(
                    out=xrow[j][0:CAP, :], out_offset=None, in_=h_rows,
                    in_offset=bass.IndirectOffsetOnAxis(ap=idx_now[0:CAP, j:j + 1], axis=0),
                    bounds_check=T - 1, oob_is_err=False).then_inc(s_gat[j], 16)

            def expert(n, j, it):
                pool.wait_ge(s_xt, n * 4 + 4)
                gather(n + 2, j)
                pool.wait_ge(s_is, n + 1)
                pool.wait_ge(s_yv, n * 4 + 4)
                held()
                pool.indirect_dma_start(
                    out=y_rows, out_offset=bass.IndirectOffsetOnAxis(ap=idx_now[0:CAP, 2 + j:3 + j], axis=0),
                    in_=yrow[0:CAP, :], in_offset=None,
                    bounds_check=2 * T - 1, oob_is_err=False).then_inc(s_sct, 16)

            pool.wait_ge(s_hst, 16 * 5)
            for j in range(2):
                pool.memset(xrow[j], 0.0).then_inc(s_z0, 1)
            pool.wait_ge(s_z0, 2)
            for j in range(2):
                gather(j, j)
            blocks(pool, expert)

        @block.vector
        def _(dve):
            tt, ts, stt = dve.tensor_tensor, dve.tensor_scalar, dve.scalar_tensor_tensor
            chain = [0]

            def link(ins):
                chain[0] += 1
                ins.then_inc(s_dve, 1)
                dve.wait_ge(s_dve, chain[0])

            dve.memset(eps, EPS).then_inc(s_set, 1)
            for c in range(4):
                dve.wait_ge(s_sq, c + 1)
                if c % 2:
                    if c == 1:
                        dve.wait_ge(s_gc, 16)
                    tt(xg[:, 4 * c:4 * c + 4, :], xg[:, 4 * c:4 * c + 4, :],
                       gmix[:, 4 * c:4 * c + 4].unsqueeze(2).to_broadcast([P, 4, T]), ALU.mult).then_inc(s_xg[1], 1)
                if c:
                    tt(sq[:, 0], sq[:, 0], sq[:, 1], ALU.add).then_inc(s_acc, 1)
                    dve.wait_ge(s_acc, c)
            link(tt(sq[:, 0, 0:2], sq[:, 0, 0:2], sq[:, 0, 2:4], ALU.add))
            tt(sq[:, 0, 0], sq[:, 0, 0], sq[:, 0, 1], ALU.add).then_inc(s_acc, 1)

            def u_out(n):
                dve.wait_ge(s_proj, n + 1)
                dst = u[:, n, 0:SEQ].rearrange("p (j c) -> p c j", j=CHUNK)
                c0 = HALF // CHUNK

                def src(a, lo, hi):
                    return a[:, lo:hi].rearrange("p (c j) -> p c j", j=CHUNK)
                tt(dst[:, 0:c0], src(pair(n)[:, 0], 0, HALF), src(rstd, 0, HALF), ALU.mult).then_inc(s_uev, 1)
                tt(dst[:, c0:NCH], src(pair(n)[:, 1], 0, SEQ - HALF), src(rstd, HALF, SEQ), ALU.mult).then_inc(s_uev, 1)
                tt(u[:, n, SEQ:T], pair(n)[:, 1, SEQ - HALF:HALF], rstd[:, SEQ:T], ALU.mult).then_inc(s_uev, 1)

            ar, ai, dt = par[:, 0], par[:, 1], par[:, 2]
            dve.wait_ge(s_lact, 1)
            tt(tmp[0], ar, dt, ALU.mult).then_inc(s_ldve, 1)
            link(tt(tmp[1], ai, dt, ALU.mult))
            link(ts(tmp[3], tmp[1], 0.5 / PI, MAGIC, ALU.mult, ALU.add))
            link(ts(tmp[3], tmp[3], MAGIC, None, ALU.subtract))
            link(stt(tmp[4], tmp[3], -TWO_PI[0], tmp[1], ALU.mult, ALU.add))
            link(stt(tmp[4], tmp[3], -TWO_PI[1], tmp[4], ALU.mult, ALU.add))
            link(stt(tmp[4], tmp[3], -TWO_PI[2], tmp[4], ALU.mult, ALU.add))
            ts(tmp[4], tmp[4], 3.1415925, -3.1415925, ALU.min, ALU.max).then_inc(s_ldve, 1)
            dve.wait_ge(s_root, 1)
            dve.reciprocal(rstd, rstd).then_inc(s_rstd, 1)
            dve.wait_ge(s_rstd, 1)
            u_out(0)
            link(tt(tmp[8], ar, ar, ALU.mult))
            link(tt(tmp[9], ai, ai, ALU.mult))
            link(tt(tmp[8], tmp[8], tmp[9], ALU.add))
            link(dve.reciprocal(tmp[9], tmp[8]))
            u_out(1)
            dve.wait_ge(s_lact, 4)
            link(tt(tmp[6], tmp[6], tmp[6], ALU.mult))
            link(ts(tmp[6], tmp[6], -2.0, 1.0, ALU.mult, ALU.add))
            tt(lre, tmp[2], tmp[6], ALU.mult)
            link(tt(lim, tmp[2], tmp[5], ALU.mult))
            link(ts(tmp[7], lre, 1.0, None, ALU.subtract))
            tt(tmp[2], tmp[7], ar, ALU.mult)
            link(tt(tmp[3], lim, ai, ALU.mult))
            link(tt(tmp[2], tmp[2], tmp[3], ALU.add))
            tt(cre, tmp[2], tmp[9], ALU.mult)
            tt(tmp[4], tmp[7], ai, ALU.mult)
            link(tt(tmp[3], lim, ar, ALU.mult))
            link(tt(tmp[3], tmp[3], tmp[4], ALU.subtract))
            tt(cim, tmp[3], tmp[9], ALU.mult).then_inc(s_ldve, 1)
            dve.wait_ge(s_ldve, 3)
            for n in range(2, 8):
                u_out(n)
                if n == 2:
                    r1, i1 = lre[:, 1024:NP], lim[:, 1024:NP]
                    dve.tensor_copy(lamp[:, 0], r1)
                    dve.tensor_copy(lamp[:, 1], i1)
                    dve.tensor_copy(coef[:, 0], cre[:, 1024:NP])
                    dve.tensor_copy(coef[:, 1], cim[:, 1024:NP])
                    a, b, c, d = (tmp[8][:, 32 * j:32 * j + 32] for j in range(4))
                    for _ in range(2):
                        tt(a, r1, r1, ALU.mult)
                        link(tt(b, i1, i1, ALU.mult))
                        link(tt(d, r1, i1, ALU.mult))
                        link(tt(c, a, b, ALU.subtract))
                        link(ts(d, d, 2.0, None, ALU.mult))
                        e, f = (tmp[9][:, 32 * j:32 * j + 32] for j in range(2))
                        dve.tensor_copy(e, c)
                        link(dve.tensor_copy(f, d))
                        r1, i1 = e, f
                    dve.tensor_copy(lam_same[:, 0], e)
                    dve.tensor_copy(lam_same[:, 1], e)
                    dve.tensor_copy(lam_cross[:, 0], f)
                    ts(lam_cross[:, 1], f, -1.0, None, ALU.mult).then_inc(s_ldve, 1)
            dve.wait_ge(s_bw, 1)
            dve.memset(xs[:, :, :, 0:1], 0.0).then_inc(s_scan, 1)
            dve.wait_ge(s_injev, 20)
            dve.wait_ge(s_ldve, 4)

            def column(c):
                return xs[:, :, :, bass.ds(c, 1)].rearrange("p r i o -> p r (i o)")

            with dve.Fori(0, NCH // 4) as it:
                for s in range(4):
                    done = it * 16 + (4 * s + 1)
                    dve.wait_ge(s_scan, done)
                    tt(scan_t[:, 0], column(it * 4 + s), lam_same, ALU.mult).then_inc(s_scan, 1)
                    tt(scan_t[:, 1, ::-1], column(it * 4 + s), lam_cross, ALU.mult).then_inc(s_scan, 1)
                    dve.wait_ge(s_scan, done + 1)
                    tt(scan_t[:, 2], scan_t[:, 0], column(it * 4 + (s + 1)), ALU.add).then_inc(s_scan, 1)
                    dve.wait_ge(s_scan, done + 3)
                    tt(column(it * 4 + (s + 1)), scan_t[:, 2], scan_t[:, 1], ALU.add).then_inc(s_scan, 1)
            dve.wait_ge(s_c, 16)
            r1, i1 = lamp[:, 0], lamp[:, 1]

            def by_sample(ap):
                return ap.unsqueeze(2).to_broadcast([P, PAIRS, NS])
            t0, t1 = scan_s[:, 0], scan_s[:, 1]
            tt(t0[:, 0], x0s[:, 0], by_sample(r1), ALU.mult)
            tt(t0[:, 1], x0s[:, 1], by_sample(r1), ALU.mult)
            tt(t1[:, 0], x0s[:, 1], by_sample(i1), ALU.mult)
            link(tt(t1[:, 1], x0s[:, 0], by_sample(i1), ALU.mult))
            link(tt(xns, xns, t0, ALU.add))
            tt(xns[:, 0], xns[:, 0], t1[:, 0], ALU.subtract)
            link(tt(xns[:, 1], xns[:, 1], t1[:, 1], ALU.add))
            dve.wait_ge(s_scan, 4 * NCH + 1)
            dve.memset(stat, 0.0).then_inc(s_state, 1)
            dve.wait_ge(s_rope, 24)

            def sample(ap):
                return ap[:, :, SEQ:T].rearrange("p h b -> p b h")
            tt(prod.rearrange("p (b h) -> p b h", b=NS), sample(q), sample(k), ALU.mult).then_inc(s_samp, 1)
            dve.tensor_copy(vsamp.rearrange("p (b h) -> p b h", b=NS), sample(v)).then_inc(s_samp, 1)

            def mask(a):
                qt = a % 4
                w = P * (qt + 1)
                dve.wait_ge(s_sco, a + 1)
                if a >= 4:
                    dve.wait_ge(s_pt, a - 3)
                tt(sc[a % 4][:, 0:w], ps[:, qt, 0:w], branch_neg[:, 512 - w:512], ALU.add).then_inc(s_msk, 1)
                dve.wait_ge(s_msk, a + 1)
                link(dve.tensor_reduce(stat[:, a:a + 1], sc[a % 4][:, 0:w], X, ALU.max))
                ts(stat[:, a:a + 1], stat[:, a:a + 1], -SCALE, None, ALU.mult).then_inc(s_mx, 1)

            def weights(a):
                w = P * (a % 4 + 1)
                dve.wait_ge(s_exp, a + 1)
                link(stt(sc[a % 4][:, 0:w], sc[a % 4][:, 0:w], 1.0, branch_n[:, 512 - w:512], ALU.mult, ALU.mult,
                         accum_out=stat[:, 32 + a % 4:33 + a % 4]))
                link(dve.reciprocal(stat[:, 36 + a % 4:37 + a % 4], stat[:, 32 + a % 4:33 + a % 4]))
                ts(sc[a % 4][:, 0:w], sc[a % 4][:, 0:w], stat[:, 36 + a % 4:37 + a % 4], None, ALU.mult).then_inc(s_p, 1)

            dve.wait_ge(s_attc, 16)
            dve.wait_ge(s_state, 1)
            mask(0)
            mask(1)
            for a in range(4 * NH):
                if a + 2 < 4 * NH:
                    mask(a + 2)
                weights(a)
            dve.wait_ge(s_lagc, 2)
            for ct in range(8):
                last = stt(lagk[:, ct, 0, :], ident, dskip[:, ct:ct + 1], lagk[:, ct, 0, :], ALU.mult, ALU.add)
            last.then_inc(s_lagd, 1)
            dve.wait_ge(s_rc, 16 * 5)
            dve.memset(row_part, 0.0)
            tt(wr, wr, gffn.unsqueeze(2).to_broadcast([P, 16, 36]), ALU.mult).then_inc(s_gwr, 1)
            dve.wait_ge(s_kout, 16)
            soft, st = smp_soft[0:64], stat[0:64]
            for n in range(8):
                dve.wait_ge(s_sig, n + 1)
                tt(z2[:, n], u[:, n], glu_t[:, n % 2], ALU.mult).then_inc(s_z2, 1)
                if n == 0:
                    dve.wait_ge(s_ssm, 1)
                    link(dve.tensor_copy(soft, ps[0:64, 7, 0:257]))
                    link(dve.tensor_reduce(st[:, 41:42], soft, X, ALU.max))
                    ts(st[:, 40:41], st[:, 41:42], -SCALE, None, ALU.mult).then_inc(s_smx, 1)
                if n == 1:
                    dve.wait_ge(s_attc, 32)
                    dve.wait_ge(s_sexp, 1)
                    link(stt(soft, soft, 1.0, smp_mult[0:64], ALU.mult, ALU.mult, accum_out=st[:, 42:43]))
                    link(dve.reciprocal(st[:, 43:44], st[:, 42:43]))
                    link(ts(soft, soft, st[:, 43:44], None, ALU.mult))
                    ts(smp_diag[0:64], ident[0:64, 0:64], soft[:, 256:257], None, ALU.mult).then_inc(s_spr, 1)
            dve.wait_ge(s_stpc, 1)
            dve.wait_ge(s_spv, NS)
            link(tt(smp_new, smp_new, vsamp, ALU.mult))
            link(tt(smp_new, ps[:, 7, 0:64], smp_new, ALU.add))
            dve.tensor_copy(sample(q), smp_new.rearrange("p (b h) -> p b h", b=NS)).then_inc(s_so, 1)
            dve.wait_ge(s_zrt, 1)
            link(dve.reciprocal(rz, rz))
            for n in range(8):
                stt(z2[:, n], z2[:, n], gso[:, n:n + 1], rz, ALU.mult, ALU.mult).then_inc(s_mix, 1)
            dve.wait_ge(s_ort, 1)
            link(dve.reciprocal(ro, ro))
            for n in range(8):
                stt(q[:, n], q[:, n], gao[:, n:n + 1], ro, ALU.mult, ALU.mult).then_inc(s_mix, 1)
            dve.wait_ge(s_x2l, 16)
            for n in range(16):
                dve.wait_ge(s_op, n + 1)
                tt(halves(x2[:, n]), pair(n), halves(x2[:, n]), ALU.add).then_inc(s_x2, 1)
            dve.wait_ge(s_rss, 20)
            dve.tensor_reduce(row_sum, row_part, X, ALU.add).then_inc(s_rrs, 1)
            link(dve.memset(logit, 0.0))
            dve.wait_ge(s_rrt, 1)
            dve.reciprocal(row_rstd, row_sum).then_inc(s_rrs, 1)
            dve.wait_ge(s_rrs, 2)
            dve.wait_ge(s_lg, 1)
            for i, n in enumerate(TOKS):
                last = stt(logit[0:n, i, :], ps[0:n, 7, 36 * i:36 * (i + 1)], row_rstd[0:n, i:i + 1], rbias[0:n],
                           ALU.mult, ALU.add)
            link(last)
            dve.tensor_copy(upper16, region("upper", P))
            dve.memset(ones16, 1.0)

            def full(ap, n):
                return ap.unsqueeze(2).to_broadcast([P, 5, n])

            def every(ap, n):
                return ap.unsqueeze(1).to_broadcast([P, 5, n])

            def first_max(src, n, m, lower, index, hot):
                link(dve.tensor_reduce(m, src, X, ALU.max))
                link(tt(lower, src, full(m, n), ALU.is_lt))
                link(stt(lower, lower, 1000.0, every(iota_b[:, 0:n], n), ALU.mult, ALU.add))
                link(dve.tensor_reduce(index, lower, X, ALU.min))
                link(tt(hot, every(iota_b[:, 0:n], n), full(index, n), ALU.is_equal))

            gmax, gidx, gsum, gate1, m1, ex, e1, m2, e2 = S5c[0], S5c[1], S5c[2], S5c[3], S5c[4], S5c[5], S5c[6], S5c[7], S5c[8]
            lg = logit[:, :, 0:NG]
            first_max(lg, NG, gmax, G20[0], gidx, G20[1])
            tt(G20[2], lg, full(gmax, NG), ALU.subtract).then_inc(s_ra, 1)
            link(ts(G20[3], G20[1], 1e30, -1e30, ALU.mult, ALU.add))
            link(tt(L32[0].rearrange("p t (g e) -> p t g e", g=NG),
                    logit[:, :, NG:].rearrange("p t (g e) -> p t g e", g=NG),
                    G20[3].unsqueeze(3).to_broadcast([P, 5, NG, EPG]), ALU.add))
            first_max(L32[0], NE, m1, L32[1], e1, L32[2])
            link(stt(L32[3], L32[2], -1e33, L32[0], ALU.mult, ALU.add))
            first_max(L32[3], NE, m2, L32[4], e2, L32[5])
            dve.wait_ge(s_ra, 2)
            link(dve.tensor_reduce(gsum, G20[2], X, ALU.add))
            link(dve.reciprocal(gate1, gsum))
            tt(ex, m2, m1, ALU.subtract).then_inc(s_ra, 1)
            tt(L32[2], L32[2], full(valid, NE), ALU.mult)
            link(tt(L32[5], L32[5], full(valid, NE), ALU.mult))
            tt(m16, L32[2], L32[5], ALU.add).then_inc(s_rb, 1)
            dve.wait_ge(s_ra, 4)
            link(ts(S5c[9], ex, 1.0, None, ALU.add))
            link(dve.reciprocal(S5c[10], S5c[9]))
            link(tt(gate_w[:, :, 0:1], gate1.unsqueeze(2), S5c[10].unsqueeze(2), ALU.mult))
            link(tt(gate_w[:, :, 1:2], gate_w[:, :, 0:1], ex.unsqueeze(2), ALU.mult))
            dve.wait_ge(s_pos, 1)
            rank, cnt, more_of, upto, base = L32[1], E32[0], E32[1], E32[2], E32[3]
            link(dve.tensor_copy(rank, ps[:, 1, 0:160].rearrange("p (t e) -> p t e", t=5)))
            link(dve.tensor_copy(cnt, ps[:, 1, 160:192]))
            link(ts(more_of, cnt, float(CAP), None, ALU.is_gt))
            for b in range(2, MAXB):
                link(stt(more_of, cnt, float(CAP * b), more_of, ALU.is_gt, ALU.add))
            link(dve.tensor_tensor_scan(upto, ones[:, 0:NE], more_of, 0.0, ALU.mult, ALU.add))
            link(tt(base, upto, more_of, ALU.subtract))
            io = iota_b[:, 0:NOV].unsqueeze(2).to_broadcast([P, NOV, NE])
            ot = [ovt, ovt2]
            link(tt(ot[0], base.unsqueeze(1).to_broadcast([P, NOV, NE]), io, ALU.is_le))
            link(tt(ot[1], upto.unsqueeze(1).to_broadcast([P, NOV, NE]), io, ALU.is_gt))
            link(tt(ot[0], ot[0], ot[1], ALU.mult))
            link(tt(ot[0], ot[0], iota_b[:, 0:NE].unsqueeze(1).to_broadcast([P, NOV, NE]), ALU.mult))
            link(dve.tensor_reduce(ovexp, ot[0], X, ALU.add))
            dve.tensor_copy(ovexp_i[:, 0:NOV], ovexp)
            link(dve.tensor_copy(ovexp_i[:, NOV:NOV + 1], upto[:, NE - 1:NE]))
            dve.memset(posblk, 0.0)
            link(dve.memset(B42[2], 0.0))
            for j, (hot, e) in enumerate(((L32[2], e1), (L32[5], e2))):
                p_, b_, w_, o_, s_ = S5c[11], S5c[12], S5c[13], S5c[14], S5c[15]
                link(tt(L32[6], hot, rank, ALU.mult))
                link(dve.tensor_reduce(p_, L32[6], X, ALU.add))
                link(tt(L32[7], hot, every(base, NE), ALU.mult))
                link(dve.tensor_reduce(o_, L32[7], X, ALU.add))
                link(ts(b_, p_, float(CAP), None, ALU.is_ge))
                for b in range(2, MAXB):
                    link(stt(b_, p_, float(CAP * b), b_, ALU.is_ge, ALU.add))
                link(stt(w_, b_, -float(CAP), p_, ALU.mult, ALU.add))
                link(tt(o_, o_, b_, ALU.add))
                link(stt(o_, o_, float(NE - 1), e, ALU.add, ALU.subtract))
                link(ts(s_, b_, 1.0, None, ALU.min))
                link(tt(o_, o_, s_, ALU.mult))
                link(tt(o_, o_, e, ALU.add))
                link(ts(w_, w_, 1.0, None, ALU.add))
                link(tt(w_, w_, valid, ALU.mult))
                link(ts(S5c[16], tok, 2.0, float(1 + j), ALU.mult, ALU.add))
                link(tt(B42[0], every(iota_b, NBLK), full(o_, NBLK), ALU.is_equal))
                link(tt(B42[1], B42[0], full(w_, NBLK), ALU.mult))
                link(tt(posblk, posblk, B42[1], ALU.add))
                link(tt(B42[1], B42[0], full(S5c[16], NBLK), ALU.mult))
                link(tt(B42[2], B42[2], B42[1], ALU.add))
            link(ts(S5c[17], tok, 1.0, None, ALU.add))
            dve.tensor_copy(rv16[:, :, :, 0:1], B42[2].unsqueeze(3))
            link(dve.tensor_copy(rv16[:, :, :, 1:2], full(S5c[17], NBLK).unsqueeze(3)))
            link(dve.memset(idx_g[:, NBLK:NBLK + 2], int(BIG) - 1))
            LG = NBLK // LISTG
            dve.wait_ge(s_hst, 16 * 5)

            def select(g):
                if g >= 2:
                    dve.wait_ge(s_lst, g - 1)
                tt(sel16[g % 2], iota_s.unsqueeze(1).unsqueeze(1).to_broadcast([P, 5, LISTG, CAP]),
                   posblk[:, :, LISTG * g:LISTG * (g + 1)].unsqueeze(3).to_broadcast([P, 5, LISTG, CAP]),
                   ALU.is_equal).then_inc(s_sel, 1)

            def lists(g):
                if 0 < g < LG - 1:
                    select(g + 1)
                dve.wait_ge(s_lst, g + 1)
                src = ps[0:CAP, 4 + g % 2, 0:2 * LISTG].rearrange("p (b c) -> p b c", c=2)
                no = none[0:CAP].rearrange("p (b c) -> p b c", c=2)
                link(ts(no, src, 0.0, BIG, ALU.is_equal, ALU.mult))
                stt(idx_s[0:CAP, LISTG * g:LISTG * (g + 1)].unsqueeze(2), src[:, :, 0:1], -1.0, no[:, :, 0:1],
                    ALU.add, ALU.add)
                stt(idx_g[0:CAP, LISTG * g:LISTG * (g + 1)].unsqueeze(2), src[:, :, 1:2], -1.0, no[:, :, 1:2],
                    ALU.add, ALU.add).then_inc(s_idx, 1)
                dve.wait_ge(s_idx, g + 1)

            def rows_turned(n):
                for g in range(4):
                    dve.wait_ge(s_xt, n * 4 + (g + 1))
                    w = min(5, 16 - 5 * g)
                    tt(xtr[:, 5 * g:5 * g + w, :], ps[:, g % 2, 0:CAP * w].rearrange("p (k n) -> p k n", n=CAP),
                       gtab[:, 5 * g:5 * g + w].unsqueeze(2).to_broadcast([P, w, CAP]), ALU.mult).then_inc(s_xte, 1)

            select(0)
            lists(0)
            for j in range(2):
                dve.tensor_copy(idx_now[0:CAP, j:j + 1], idx_g[0:CAP, j:j + 1]).then_inc(s_ig, 1)
            select(1)
            lists(1)
            lists(2)
            dve.wait_ge(s_gt, 16)
            rows_turned(0)
            for g in range(3, LG):
                lists(g)

            def expert(n, j, it):
                dve.wait_ge(s_gat[j], it * 16 + 16)
                dve.tensor_copy(idx_now[0:CAP, j:j + 1], idx_g[0:CAP, bass.ds(n + 2, 1)]).then_inc(s_ig, 1)
                if type(n) is not int:
                    dve.wait_ge(s_sct, n * 16 - 16)
                dve.tensor_copy(idx_now[0:CAP, 2 + j:3 + j], idx_s[0:CAP, bass.ds(n, 1)]).then_inc(s_is, 1)
                dve.wait_ge(s_si, n + 1)
                dve.wait_ge(s_up, n + 1)
                tt(actt.rearrange("p m n -> p (m n)"), sil, ps[:, 3, 0:4 * CAP], ALU.mult).then_inc(s_ac, 1)
                rows_turned(n + 1)

            blocks(dve, expert)
            dve.wait_ge(s_gf, 16)
            for i, n in enumerate(TOKS):
                b = i
                dve.wait_ge(s_finl[i], 32)
                for j in range(2):
                    ins = stt(fx[b][0:n], fy[b][0:n, j, :], gate_w[0:n, i, j:j + 1], fx[b][0:n], ALU.mult, ALU.add)
                    if j == 0:
                        link(ins)
                ins.then_inc(s_fin, 1)
                dve.wait_ge(s_fr, i + 1)
                link(dve.reciprocal(fstat[0:n, 1, i:i + 1], fstat[0:n, 0, i:i + 1]))
                stt(fx[b][0:n], fx[b][0:n], fstat[0:n, 1, i:i + 1], fg[0:n], ALU.mult, ALU.mult).then_inc(s_fo, 1)


def key_positions(past):
    import numpy as np
    dist = [d for d in range(1, past + 1)
            if d <= 128 or (d % 4 == 0 and d <= 512) or (d % 16 == 0 and d <= 2048)]
    many = [(d <= 128) + (d % 4 == 0 and d <= 512) + (d % 16 == 0 and d <= 2048) for d in dist]
    assert len(dist) == KEYS
    return past - np.array(dist), np.array(many + [3], np.float32)


def constants():
    import numpy as np
    c = {}
    c["c_mats"] = np.concatenate([np.eye(P), np.ones((P, P))], 1).astype(np.float32)
    c["c_upper"] = np.triu(np.ones((P, P)), 1).astype(np.float32)
    half = DH // 2
    pos = np.concatenate([np.arange(SEQ), np.full(NS, 1024)]).astype(np.float32)
    inv = np.float32(10000.0) ** (-np.arange(half, dtype=np.float32) / np.float32(half))
    ang = (pos[:, None] * inv[None, :].astype(np.float32)).astype(np.float32).astype(np.float64)
    cs, sn = np.cos(ang).T, np.sin(ang).T
    c["c_rope"] = np.concatenate([np.concatenate([cs, cs]), np.concatenate([-sn, sn])], 1).astype(np.float32)
    d = (P * np.arange(3, -1, -1)[:, None, None] + np.arange(P)[None, :, None] - np.arange(P)[None, None, :])
    many = ((d >= 0) & (d <= 128)).astype(np.float32)
    for w, s in ((512, 4), (2048, 16)):
        many += (d >= 0) & (d <= w) & (d % s == 0)
    many = many.transpose(1, 0, 2).reshape(P, 512)
    c["c_branch"] = np.concatenate([many, np.where(many > 0, 0.0, -1e30)], 1).astype(np.float32)
    c["c_sample"] = np.tile(key_positions(1024)[1], (64, 1)).astype(np.float32)
    tok = P * np.arange(5)[None, :] + np.arange(P)[:, None]
    c["c_router"] = np.concatenate([np.tile(np.arange(NBLK), (P, 1)), np.tile(np.arange(1, CAP + 1), (P, 1)),
                                    tok < T, np.minimum(tok, T)], 1).astype(np.float32)
    return c


def host_inputs(a):
    import numpy as np
    d = constants()
    x = np.concatenate([a["x_prompt"][0], a["x_sample"][:, 0]], 0)
    d["x_cols"] = x.T.reshape(16, P, T).transpose(1, 0, 2)
    d["w_in"] = a["w_in"][0].reshape(16, P, 32, P).transpose(2, 1, 0, 3).reshape(32, P, DM)
    d["w_glu"] = a["w_glu"][0].reshape(8, P, 8, P).transpose(2, 1, 0, 3).reshape(8, P, 1024)
    d["w_out"] = a["w_out"][0].reshape(16, P, 16, P).transpose(2, 1, 0, 3).reshape(16, P, DM)
    g, n, p = 64, 64, 16
    cols = lambda v: v.reshape(-1, P).T
    d["g_cols"] = np.concatenate([cols(a["g_mix_norm"][0]), cols(a["g_ssm_out"][0]), cols(a["g_attn_out"][0]),
                                  cols(a["g_ffn_norm"][0]), cols(a["ssm_d"][0].reshape(-1))], 1)
    par = []
    for v in (a["ssm_a_re"][0], a["ssm_a_im"][0], np.broadcast_to(a["ssm_log_dt"][0][:, None], (g, n))):
        chan = v.reshape(8, 4, 2 * n).transpose(1, 0, 2)
        chan = np.repeat(chan[:, None], 32, 1).reshape(P, 1024)
        par.append(np.concatenate([chan, v.reshape(PAIRS, 2 * n).T], 1))
    d["ssm_par"] = np.stack(par, 1)

    def chan_blocks(b):
        out = np.zeros((4, 2, p, 8, 2, n), np.float32)
        b = b.reshape(8, 4, 2, n, p)
        for s in range(2):
            out[:, s, :, :, s, :] = b[:, :, s].transpose(1, 3, 0, 2)
        return out.reshape(P, 1024)

    def state_blocks(b):
        out = np.zeros((2, n, PAIRS, 2, p), np.float32)
        b = b.reshape(PAIRS, 2, n, p)
        for s in range(2):
            out[s, :, :, s] = b[:, s].transpose(1, 0, 2)
        return out.reshape(P, PAIRS, 32)

    d["ssm_b_chan"] = np.stack([chan_blocks(a["ssm_b_re"][0]), chan_blocks(a["ssm_b_im"][0])], 1)
    d["ssm_b_state"] = np.stack([state_blocks(a["ssm_b_re"][0]), state_blocks(a["ssm_b_im"][0])], 1)
    d["ssm_c"] = np.stack([state_blocks(a["ssm_c_re"][0].transpose(0, 2, 1)),
                           state_blocks(a["ssm_c_im"][0].transpose(0, 2, 1))], 1)
    st = lambda s: s[0].reshape(NS, PAIRS, P).transpose(2, 1, 0)
    d["ssm_x0"] = np.stack([st(a["state_ssm_re"]), st(a["state_ssm_im"])], 1)
    rows = key_positions(a["cache_k"].shape[2])[0]
    ck, cv = a["cache_k"][0][:, rows], a["cache_v"][0][:, rows]
    d["k_cache"] = ck.transpose(0, 3, 2, 1).reshape(NS, P, DM)
    d["v_cache"] = cv.reshape(NS, 2, P, 1024).transpose(0, 2, 1, 3).reshape(NS, P, DM)
    wr = np.concatenate([a["w_router_group"][0], a["w_router_expert"][0].reshape(DM, NE)], 1)
    d["w_router"] = wr.reshape(16, P, 36).transpose(1, 0, 2).reshape(P, 576)
    d["b_router"] = np.concatenate([a["b_router_group"][0], a["b_router_expert"][0].reshape(-1)])[None]
    d["g_ffn"], d["g_final"] = a["g_ffn_norm"], a["g_final"][None]
    d["w_gate"], d["w_up"], d["w_down"] = a["w_expert_gate"][0], a["w_expert_up"][0], a["w_expert_down"][0]
    return {f"{k}_in": np.ascontiguousarray(v) for k, v in d.items()}


OUTS = {"y_out": (T, DM), "k_out": (P, NH, T), "v_out": (P, NH, T), "state_out": (P, 2, PAIRS, 9)}


def kernel(**inputs):
    import numpy as np
    import concourse.bacc as bacc
    from concourse.bass_utils import run_bass_kernel_spmd
    arrays = host_inputs({name: np.asarray(v) for name, v in inputs.items()})
    nc = bacc.Bacc("TRN2", target_bir_lowering=False, num_devices=1)
    t = {}
    for name, v in arrays.items():
        t[name[:-3]] = nc.dram_tensor(name, v.shape, F32, kind="ExternalInput").ap()
    for name, shape in OUTS.items():
        t[name] = nc.dram_tensor(name, shape, F32, kind="ExternalOutput").ap()
    build(nc, t)
    r = run_bass_kernel_spmd(nc, [arrays], core_ids=[0]).results[0]
    y = r["y_out"]
    kv = []
    for name in ("k_out", "v_out"):
        m = np.asarray(r[name]).transpose(2, 1, 0)
        kv.append((m[:SEQ][None, None], m[SEQ:][None, :, None]))
    states = np.asarray(r["state_out"]).transpose(3, 1, 2, 0).reshape(9, 2, 64, 64)
    return (y[:SEQ][None], y[SEQ:][:, None], kv[0][0], kv[1][0], states[0:1, 0][None], states[0:1, 1][None],
            kv[0][1], kv[1][1], states[1:, 0][None], states[1:, 1][None])
```

```python
from contextlib import ExitStack

import concourse.bass as bass
from concourse import mybir

F32 = mybir.dt.float32
F16 = mybir.dt.float16
U32 = mybir.dt.uint32
ALU = mybir.AluOpType
ACT = mybir.ActivationFunctionType
X = mybir.AxisListType.X

P = 128
DM = 2048
SEQ, NS = 512, 8
T = SEQ + NS
HALF = T // 2
NH, DH = 8, 128
PAIRS = 32
CHUNK = 4
NCH = SEQ // CHUNK
KEYS = 256
NE, EPG, NG = 32, 8, 4
CAP = 96
NOV = (2 * T) // CAP
NBLK = NE + NOV
LISTG = 7
EPS = 1e-6
SCALE = DH ** -0.5
MAGIC = 12582912.0
PI = 3.14159265358979
TWO_PI = (6.28125, 0.0019350051879882812, 3.019916e-07)
BIG = 4096.0


def layout():
    at, off = {}, 0
    for name, n in (("ident", P), ("ones", P), ("rstd", T), ("cos", T), ("sin", T), ("gmix", 16), ("gso", 8),
                    ("gao", 8), ("gffn", 16), ("dskip", 8), ("lr", 64), ("li", 64), ("lamp", 64), ("coef", 64),
                    ("vsamp", 64), ("eps", 1), ("stat", 64), ("upper", P)):
        at[name] = off
        off += n
    off = 2600
    for name, n in (("A", 16 * T), ("R", 11664), ("W", 4096), ("U", 8 * T), ("Q", 8 * T), ("K", 8 * T),
                    ("V", 8 * T), ("X", 9792)):
        at[name] = off
        off += n
    at["end"] = off
    return at


def build(nc, t):
    at = layout()
    ctx = ExitStack()
    with ctx:
        arena_t = ctx.enter_context(nc.sbuf_tensor("arena", [P, at["end"]], F32))
        psum_t = ctx.enter_context(nc.psum_tensor("psum", [P, 8 * 512], F32))
        arena = arena_t[:, :]
        ps = psum_t[:, :].rearrange("p (b n) -> p b n", b=8)

        def sem(name):
            return ctx.enter_context(nc.semaphore(name))

        def view(off, n):
            return arena[:, off:off + n]

        def region(name, n, shift=0):
            return view(at[name] + shift, n)

        def dram(name, shape):
            return nc.dram_tensor(name, shape, F32, kind="Internal").ap()

        h_rows = dram("h_rows", (T, DM))
        x2_rows = dram("x2_rows", (T, DM))
        y_rows = dram("y_rows", (2 * T, DM))

        ident, ones = region("ident", P), region("ones", P)
        rstd, cos, sin = region("rstd", T), region("cos", T), region("sin", T)
        gmix, gso, gao, gffn = region("gmix", 16), region("gso", 8), region("gao", 8), region("gffn", 16)
        dskip = region("dskip", 8)
        lam_same = region("lr", 64).rearrange("p (r i) -> p r i", r=2)
        lam_cross = region("li", 64).rearrange("p (r i) -> p r i", r=2)
        lamp = region("lamp", 64).rearrange("p (r i) -> p r i", r=2)
        coef = region("coef", 64).rearrange("p (r i) -> p r i", r=2)
        vsamp = region("vsamp", 64).rearrange("p (b h) -> p b h", b=NS)
        eps = region("eps", 1)
        xg = region("A", 16 * T).rearrange("p (k n) -> p k n", k=16)
        wring = region("W", 4096).rearrange("p (s k n) -> p s k n", s=2, k=16)
        u = region("U", 8 * T).rearrange("p (c n) -> p c n", c=8)
        q = region("Q", 8 * T).rearrange("p (c n) -> p c n", c=8)
        k = region("K", 8 * T).rearrange("p (c n) -> p c n", c=8)
        v = region("V", 8 * T).rearrange("p (c n) -> p c n", c=8)
        xs = region("X", 64 * (NCH + 1)).rearrange("p (r i n) -> p r i n", r=2, i=PAIRS)
        x0s = region("X", 512, 8256).rearrange("p (r i n) -> p r i n", r=2, i=PAIRS)
        xns = region("X", 512, 8768).rearrange("p (r i n) -> p r i n", r=2, i=PAIRS)
        sq = region("X", 4160).rearrange("p (s k n) -> p s k n", s=2, k=4)
        braw = region("X", 2048, 4160).rearrange("p (r n) -> p r n", r=2)
        bw = region("Q", 8192).rearrange("p (k r c n) -> p k r c n", k=CHUNK, r=2, c=8)
        ust = region("R", 4352, 5376).rearrange("p (c r n) -> p c r n", c=8, r=4)
        bws = [region("V", 2048, 2048 * j).rearrange("p (c r m) -> p c r m", c=4, r=4) for j in range(2)]
        NP = 1056
        par = region("R", 3 * NP).rearrange("p (a n) -> p a n", a=3)
        tmp = [region("R", NP, (3 + j) * NP) for j in range(8)] + [region("V", NP, j * NP) for j in range(3)]
        lre, lim, cre, cim = tmp[0], tmp[1], tmp[2], tmp[3]
        rope_in = region("R", 4 * T).rearrange("p (s r n) -> p s r n", s=2, r=2)
        rope_t = region("R", 2 * T, 4 * T).rearrange("p (s n) -> p s n", s=2)
        cosr, sinr = region("R", T, 6 * T), region("R", T, 7 * T)
        scan_t = region("R", 192, 8 * T).rearrange("p (s r i) -> p s r i", s=3, r=2)
        scan_s = region("R", 1024, 8 * T + 192).rearrange("p (s r i n) -> p s r i n", s=2, r=2, i=PAIRS)
        cw = region("A", 10240).rearrange("p (k r i m) -> p k r i m", k=CHUNK + 1, r=2, i=PAIRS)
        lagk = region("A", 4096, 10240).rearrange("p (c j m) -> p c j m", c=8, j=CHUNK)
        bst = region("V", 2048).rearrange("p (r i m) -> p r i m", r=2, i=PAIRS)
        bt = [region("V", 1024, 2048 + 1024 * j).rearrange("p (i m) -> p i m", i=PAIRS) for j in range(2)]
        tail = at["A"] + 14336
        branch_n, branch_neg = view(tail, 512), view(tail + 512, 512)
        sc = [view(o, 512) for o in (tail + 1024, tail + 1536, tail + 4096, tail + 4608)]
        pt = view(tail + 2048, 2048).rearrange("p (a j n) -> p a j n", a=4, j=4)
        stat = region("stat", 64)
        vrows = region("W", 4096).rearrange("p (j n) -> p j n", j=4)
        HK = KEYS // 2
        kch = [view(tail + 1024 + 2048 * j, 2048).rearrange("p (k d) -> p k d", k=16) for j in range(2)]
        vch = [region("V", 2048, 2048 * j).rearrange("p (d k) -> p d k", d=16) for j in range(2)]
        smp = tail + 5120
        smp_q, smp_p = view(smp, DH), view(smp + DH, HK + 1)
        smp_const = view(smp + 257, HK + 1 + 64)
        smp_mult, pairs = smp_const[:, 0:HK + 1], smp_const[:, HK + 1:]
        assert smp + 257 + HK + 65 <= at["W"]
        soff = at["A"] + 16384
        smp_ex = [view(soff, DH), view(soff + 128, DH)]
        smp_k, smp_v = view(soff + 256, DH), view(soff + 384, DH)
        smp_o = view(soff + 512, DH + 1)
        smp_m = view(soff + 642, P)
        smp_n = view(soff + 770, DH)
        glu_t = view(soff + 924, 2 * T).rearrange("p (s n) -> p s n", s=2)
        glu_q = view(soff + 1964, 2 * T).rearrange("p (s n) -> p s n", s=2)
        z2 = k
        rz, ro = view(soff + 3004, T), region("rstd", T)
        x2 = xg
        ms = at["R"]
        x2row = view(ms, 4 * DM).rearrange("p (i n) -> p i n", i=4)
        x2_of = [x2row[:, i, :] for i in range(4)] + [region("V", DM, 512)]
        rowjunk = region("V", 512)
        ro_at = at["cos"]
        xrow = [view(ms + DM * j, DM) for j in range(2)]
        xtr = view(ms + 4096, 16 * CAP).rearrange("p (k n) -> p k n", k=16)
        sil = view(ms + 5632, 4 * CAP)
        actt = view(ms + 6016, 4 * CAP).rearrange("p (m n) -> p m n", m=4)
        yrow = view(ms + 6400, DM)
        slots = [at["R"] + 9424 + 8192 * j for j in range(4)] + [at["A"]]
        wg = [view(slots[0], 8192).rearrange("p (k n) -> p k n", k=16),
              view(slots[3], 8192).rearrange("p (k n) -> p k n", k=16)]
        wu = [view(slots[1], 8192).rearrange("p (k n) -> p k n", k=16),
              view(slots[4], 8192).rearrange("p (k n) -> p k n", k=16)]
        wd = view(slots[2], 8192).rearrange("p (k n) -> p k n", k=4)

        s_x = [sem(f"x_loaded{c}") for c in range(4)]
        s_const = sem("const_loaded")
        s_gc = sem("gains_loaded")
        s_par = sem("params_loaded")
        s_braw = sem("b_loaded")
        s_set = sem("constants_set")
        s_w = [sem(f"w_loaded{j}") for j in range(2)]
        s_sq = sem("squares_ready")
        s_xg = [sem(f"xg_ready{j}") for j in range(2)]
        s_part = sem("first_tile_parts")
        s_acc = sem("squares_added")
        s_ss = sem("sumsq_ready")
        s_root = sem("root_ready")
        s_rstd = sem("rstd_ready")
        s_proj = sem("proj_ready")
        s_uev = sem("u_ready")
        s_qev = sem("qkv_evacuated")
        s_rope = sem("qkv_ready")
        s_dve = sem("dve_chain")
        s_pool = sem("pool_chain")
        s_lact = sem("lambda_act")
        s_ldve = sem("lambda_dve")
        s_bw = sem("inject_weights_ready")
        s_bs, s_us = [sem(f"inject_weights_stacked{j}") for j in range(4)], sem("u_stacked")
        s_zu = sem("stack_zeroed")
        s_inj = sem("inject_ready")
        s_injev = sem("inject_evacuated")
        s_scan = sem("scan_steps")
        s_state = sem("states_ready")
        s_out = sem("outputs_stored")
        s_kout, s_vout = sem("k_stored"), sem("v_stored")
        s_c = sem("c_loaded")
        s_cw = sem("c_weights_ready")
        s_vr, s_vrev = sem("v_transposed"), sem("v_rows_ready")
        s_attc = sem("attention_const_loaded")
        s_sco, s_msk, s_mx, s_exp = sem("scores_ready"), sem("scores_masked"), sem("max_ready"), sem("exp_ready")
        s_p, s_pt, s_ptev = sem("probs_ready"), sem("probs_transposed"), sem("probs_t_ready")
        s_o, s_oev = sem("o_ready"), sem("o_evacuated")
        s_lag, s_lagc, s_lagd = sem("lag_psum_ready"), sem("lag_copied"), sem("lag_ready")
        s_y, s_z = sem("y_ready"), sem("z_ready")
        s_kch = [sem(f"cached_keys{j}") for j in range(2)]
        s_vch = [sem(f"cached_values{j}") for j in range(2)]
        s_sc, s_ku, s_vu = sem("sample_const_loaded"), sem("cached_keys_used"), sem("cached_values_used")
        s_gw = [sem(f"w_glu_loaded{j}") for j in range(4)]
        s_ex, s_rows = sem("sample_columns_doubled"), sem("sample_rows_psum")
        s_vs = sem("sample_values_copied")
        s_mh, s_mt = sem("sample_max_sbuf"), sem("sample_max_psum")
        s_smx, s_sexp = sem("sample_max"), sem("sample_exp")
        s_spr, s_stp, s_so = sem("sample_o_sbuf"), sem("sample_o_psum"), sem("sample_o")
        s_glu, s_sig, s_z2 = sem("glu_ready"), sem("sigmoid_ready"), sem("z2_ready")
        s_zsq, s_osq = sem("z_squares"), sem("o_squares")
        s_zss, s_oss = sem("z_sumsq"), sem("o_sumsq")
        s_zrt, s_ort = sem("z_root"), sem("o_root")
        s_mix = sem("mix_ready")
        s_x2l = sem("x_reloaded")
        s_op, s_x2 = sem("outproj_ready"), sem("x2_ready")
        s_rc = sem("router_const_loaded")
        s_gwr = sem("router_weights_ready")
        s_tr, s_trev = sem("x2_transposed"), sem("x2_rows_ready")
        s_rss, s_rrt, s_rrs = sem("row_sumsq"), sem("row_root"), sem("row_rstd")
        s_hr = sem("h_row_ready")
        s_x2st, s_hst = sem("x2_stored"), sem("h_stored")
        s_lg = sem("logits_psum")
        s_ra, s_rb = sem("router_act"), sem("router_dve")
        s_pos = sem("positions_psum")
        s_sel, s_lst, s_idx = sem("selection_ready"), sem("lists_psum"), sem("indices_ready")
        s_e = {n: [sem(f"{n}_loaded{j}") for j in range(c)] for n, c in (("g", 2), ("u", 2), ("d", 1))}
        s_ig, s_is = sem("gather_index_ready"), sem("scatter_index_ready")
        s_gat, s_sct = [sem(f"rows_gathered{j}") for j in range(2)], sem("rows_scattered")
        s_xt, s_xte = sem("x_transposed"), sem("x_t_ready")
        s_ga, s_up, s_si, s_ac = sem("gate_psum"), sem("up_psum"), sem("silu_ready"), sem("act_ready")
        s_dn, s_yv = sem("down_psum"), sem("y_ready_rows")
        s_z0 = sem("rows_zeroed")
        s_fin, s_fq, s_fr, s_fo = sem("final_loaded"), sem("final_sumsq"), sem("final_root"), sem("final_ready")
        s_fst = sem("final_stored")
        s_finl = [sem(f"final_loaded{j}") for j in range(5)]
        s_held = sem("pool_waited")
        s_gf = sem("g_final_loaded")
        s_gt = sem("g_ffn_table_loaded")

        class Cols:
            def __init__(self, base):
                self.at = base

            def __call__(self, n):
                self.at += n
                return view(self.at - n, n)

        col = Cols(ro_at)
        row_part = col(20).rearrange("p (i g) -> p i g", g=4)
        row_sum, row_rstd = col(5), col(5)
        wr = col(576).rearrange("p (k n) -> p k n", k=16)
        rbias = col(36)
        iota_b, iota_s, valid, tok = col(NBLK), col(CAP), col(5), col(5)
        router_const = view(ro_at + 642, NBLK + CAP + 10)
        logit = col(180).rearrange("p (t n) -> p t n", t=5)
        keep = Cols(ms + 6400 + DM)
        gate_w = keep(10).rearrange("p (t j) -> p t j", t=5)
        idx_g = keep(NBLK + 2).bitcast(U32)
        idx_s = keep(NBLK + 1).bitcast(U32)
        idx_now = keep(4).bitcast(U32)
        none = keep(2 * LISTG)
        gtab = keep(16)
        ovexp = keep(NOV)
        ovexp_i = keep(NOV + 1).bitcast(U32)
        posblk = keep(5 * NBLK).rearrange("p (t b) -> p t b", t=5)
        rv16 = keep(5 * NBLK).bitcast(F16).rearrange("p (t b c) -> p t b c", t=5, c=2)
        upper16 = keep(64).bitcast(F16)
        ones16 = keep(64).bitcast(F16)
        m16 = keep(80).bitcast(F16).rearrange("p (t e) -> p t e", t=5)
        assert keep.at <= ms + 9424, keep.at - ms
        rt = Cols(at["A"])
        SELN = 5 * LISTG * CAP // 2
        sel16 = [c.bitcast(F16).rearrange("p (t b s) -> p t b s", t=5, b=LISTG)
                 for c in (rt(SELN), rt(SELN), yrow[:, 0:SELN])]
        in_group, elow, rest, elow2, rank = (rt(160).rearrange("p (t e) -> p t e", t=5) for _ in range(5))
        hot = rt(320).rearrange("p (c e) -> p c e", e=NE)
        chosen = rt(10)
        C10 = [rt(10) for _ in range(5)]
        wide_e = [rt(320).rearrange("p (c e) -> p c e", e=NE) for _ in range(2)]
        wide_b = [rt(10 * NBLK).rearrange("p (c b) -> p c b", b=NBLK) for _ in range(2)]
        gmax, gidx, gsum, gate1, m1, m2, ex, ex_sum, gate_1st, tok1 = (rt(5) for _ in range(10))
        cnt, more_of, upto, base = (rt(NE) for _ in range(4))
        glow, ghot, gexp, gmask = (rt(20).rearrange("p (t g) -> p t g", t=5) for _ in range(4))
        ovt, ovt2 = (rt(NOV * NE).rearrange("p (o e) -> p o e", o=NOV) for _ in range(2))
        assert rt.at <= at["R"]
        assert col.at <= at["gmix"]

        glu_w = region("W", 4096).rearrange("p (s n) -> p s n", s=4)
        ujc = u[:, :, 0:SEQ].rearrange("p t (j c) -> p t j c", j=CHUNK)
        yjc = [ps[:, 2 * b, :].rearrange("p (j c) -> p j c", j=CHUNK) for b in range(2)]
        fx = [view(slots[0] + 6144 * b, DM) for b in range(5)]
        fy = [view(slots[0] + 6144 * b + DM, 2 * DM).rearrange("p (j n) -> p j n", j=2) for b in range(5)]
        fjunk, fg = view(slots[4], DM), view(slots[4] + DM, DM)
        fstat = stat[:, 0:10].rearrange("p (s n) -> p s n", s=2)
        TOKS = [P, P, P, P, NS]

        def pair(n):
            return ps[:, 2 * (n % 2):2 * (n % 2) + 2, 0:HALF]

        def halves(ap):
            return ap.rearrange("p (h n) -> p h n", h=2)

        def overflow_blocks(eng):
            eng.wait_ge(s_idx, NBLK // LISTG)
            return eng.value_load(ovexp_i[0:1, NOV:NOV + 1], min_val=0, max_val=NOV)

        def first(n):
            return type(n) is int and n == 0

        def blocks(eng, body):
            for j in range(2):
                body(j, j, 0)
            with eng.Fori(1, NE // 2) as it:
                for j in range(2):
                    body(it * 2 + j, j, it)
            more = overflow_blocks(eng)
            with eng.Fori(NE // 2, NBLK // 2) as it:
                for j in range(2):
                    with eng.If(it * 2 + (j - NE) < more):
                        body(it * 2 + j, j, it)
            return more

        block = ctx.enter_context(nc.Block())

        @block.sync
        def _(sp):
            def load_w(n, src):
                sp.dma_start(wring[:, n % 2].rearrange("p k n -> p (k n)"), src).then_inc(s_w[n % 2], 16)

            for c in range(4):
                sp.dma_start(xg[:, 4 * c:4 * c + 4, :], t["x_cols"][:, 4 * c:4 * c + 4, :]).then_inc(s_x[c], 16)
                if c == 0:
                    sp.dma_start(region("gmix", 56), t["g_cols"]).then_inc(s_gc, 16)
                    load_w(0, t["w_in"][0])
                if c == 1:
                    sp.dma_start(view(0, 2 * P), t["c_mats"]).then_inc(s_const, 16)
            load_w(1, t["w_in"][1])
            sp.dma_start(par, t["ssm_par"]).then_inc(s_par, 16)
            sp.dma_start(x0s, t["ssm_x0"]).then_inc(s_c, 16)
            sp.dma_start(view(at["cos"], 2 * T), t["c_rope"]).then_inc(s_rc, 16)
            sp.dma_start(braw, t["ssm_b_chan"]).then_inc(s_braw, 16)
            for n in range(2, 4):
                sp.wait_ge(s_proj, n - 1)
                load_w(n, t["w_in"][n])

            def load_tiles(a, b, keys=None):
                with sp.Fori(a, b) as it:
                    for j in range(2):
                        sp.wait_ge(s_proj, it * 2 + (j - 1))
                        sp.dma_start(wring[:, j].rearrange("p k n -> p (k n)"),
                                     t["w_in"][bass.ds(it * 2 + j, 1)].rearrange("o p n -> (o p) n")
                                     ).then_inc(s_w[j], 16)
                        if keys is not None:
                            if a > keys:
                                sp.wait_ge(s_ku, it * 2 + (j - 2 * keys - 1))
                            sp.dma_start(kch[j].rearrange("p k d -> p (k d)"),
                                         t["k_cache"][bass.ds(it * 2 + (j - 2 * keys), 1)].rearrange(
                                             "o p n -> (o p) n")).then_inc(s_kch[j], 16)

            load_tiles(2, 8)
            sp.wait_ge(s_inj, 24)
            sp.dma_start(view(tail, 1024), t["c_branch"]).then_inc(s_attc, 16)
            sp.dma_start(smp_const, t["c_sample"]).then_inc(s_sc, 16)
            load_tiles(8, 11)
            load_tiles(11, 12, 11)
            load_tiles(12, 15, 11)
            load_tiles(15, 16)
            sp.wait_ge(s_rope, 16)
            sp.dma_start(t["k_out"], k).then_inc(s_kout, 16)
            sp.wait_ge(s_rope, 24)
            sp.dma_start(t["v_out"], v).then_inc(s_vout, 16)
            sp.dma_start(view(ro_at + 30, 576), t["w_router"]).then_inc(s_rc, 16)
            sp.dma_start(rbias, t["b_router"].to_broadcast([P, 36])).then_inc(s_rc, 16)
            sp.dma_start(router_const, t["c_router"]).then_inc(s_rc, 16)
            sp.dma_start(region("upper", P), t["c_upper"]).then_inc(s_rc, 16)
            sp.wait_ge(s_proj, 32)
            sp.wait_ge(s_state, 1)
            sp.dma_start(cw[:, 0], t["ssm_c"]).then_inc(s_c, 16)
            sp.wait_ge(s_vout, 16)
            sp.wait_ge(s_vr, 8)
            sp.wait_ge(s_vs, 1)
            sp.dma_start(bst, t["ssm_b_state"]).then_inc(s_c, 16)
            with nc.allow_non_contiguous_dma(reason="one column per state"):
                for r in range(2):
                    sp.dma_start(t["state_out"][:, r, :, 0:1], xs[:, r, :, NCH:NCH + 1]).then_inc(s_out, 16)
                    sp.dma_start(t["state_out"][:, r, :, 1:9], xns[:, r]).then_inc(s_out, 16)
            sp.wait_ge(s_lag, 1)

            def load_values(c):
                sp.dma_start(vch[c % 2].rearrange("p d k -> p (d k)"), t["v_cache"][c]).then_inc(s_vch[c % 2], 16)

            for c in range(2):
                load_values(c)
            sp.wait_ge(s_o, NH)
            for n in range(4):
                sp.dma_start(glu_w[:, n], t["w_glu"][n]).then_inc(s_gw[n], 16)
            for c in range(2, 8):
                sp.wait_ge(s_vu, c - 1)
                load_values(c)
            sp.wait_ge(s_y, 8)
            sp.dma_start(x2, t["x_cols"]).then_inc(s_x2l, 16)
            for n in range(4, 8):
                sp.wait_ge(s_glu, n - 3)
                sp.dma_start(glu_w[:, n % 4], t["w_glu"][n]).then_inc(s_gw[n % 4], 16)
            for n in range(2):
                sp.wait_ge(s_glu, 6 + 2 * n)
                load_w(n, t["w_out"][n])

            def store_x2(g):
                c = slice(512 * g, 512 * (g + 1))
                sp.wait_ge(s_trev, 5 * (g + 1))
                sp.dma_start(x2_rows[0:SEQ, c].rearrange("(i p) n -> p i n", p=P), x2row[:, 0:4, c]
                             ).then_inc(s_x2st, 16)
                sp.dma_start(x2_rows[SEQ:T, c], x2_of[4][0:NS, c]).then_inc(s_x2st, 16)

            for n in range(2, 16):
                if n % 4 == 3 and n > 4:
                    store_x2(n // 4 - 1)
                sp.wait_ge(s_op, n - 1)
                load_w(n, t["w_out"][n])
            store_x2(3)

            def gate(e, j):
                sp.dma_start(wg[j], t["w_gate"][bass.ds(e, 1)].rearrange("o (p k) n -> (o p) k n", k=16)
                             ).then_inc(s_e["g"][j], 16)

            def up(e, j):
                sp.dma_start(wu[j], t["w_up"][bass.ds(e, 1)].rearrange("o (p k) n -> (o p) k n", k=16)
                             ).then_inc(s_e["u"][j], 16)

            def down(e):
                sp.dma_start(wd, t["w_down"][bass.ds(e, 1)].rearrange("o (k p) n -> p (o k) n", k=4)
                             ).then_inc(s_e["d"][0], 16)

            for i, n in enumerate(TOKS):
                sp.wait_ge(s_hr, i + 1)
                sp.dma_start(h_rows[P * i:P * i + n, :], x2_of[i][0:n]).then_inc(s_hst, 16)
            sp.dma_start(gtab, t["g_ffn"].rearrange("o (p k) -> (o p) k", k=16)).then_inc(s_gt, 16)
            sp.wait_ge(s_op, 16)
            gate(0, 0)
            for j in range(2):
                sp.wait_ge(s_gat[j], 16)
            up(0, 0)
            down(0)
            gate(1, 1)
            sp.wait_ge(s_lst, NBLK // LISTG)
            up(1, 1)

            def loads(m, j):
                sp.wait_ge(s_ga, m + 1)
                gate(m + 2, j)
                sp.wait_ge(s_up, m + 1)
                up(m + 2, j)
                sp.wait_ge(s_dn, m * 4 + 4)
                down(m + 1)

            with sp.Fori(0, NE // 2 - 1) as it:
                for j in range(2):
                    loads(it * 2 + j, j)
            sp.wait_ge(s_dn, 4 * (NE - 1))
            down(NE - 1)
            more = overflow_blocks(sp)
            with sp.Fori(NE // 2, NBLK // 2) as it:
                for j in range(2):
                    with sp.If(it * 2 + (j - NE) < more):
                        e = sp.value_load(ovexp_i[0:1, bass.ds(it * 2 + (j - NE), 1)], min_val=0, max_val=NE - 1)
                        sp.wait_ge(s_ga, it * 2 + (j - 1))
                        gate(e, j)
                        sp.wait_ge(s_up, it * 2 + (j - 1))
                        up(e, j)
                        sp.wait_ge(s_dn, it * 8 + 4 * j)
                        down(e)
            sp.wait_ge(s_dn, more * 4 + 4 * NE)
            sp.wait_ge(s_x2st, 16 * 8)
            sp.dma_start(fg, t["g_final"].to_broadcast([P, DM])).then_inc(s_gf, 16)
            for i, n in enumerate(TOKS):
                sp.dma_start(fx[i][0:n], x2_rows[P * i:P * i + n, :]).then_inc(s_finl[i], 16)
            sp.wait_ge(s_sct, more * 16 + 16 * NE)
            for i, n in enumerate(TOKS):
                sp.dma_start(fy[i][0:n].rearrange("p j n -> p (j n)"),
                             y_rows[2 * P * i:2 * P * i + 2 * n, :].rearrange("(p j) n -> p (j n)", j=2)
                             ).then_inc(s_finl[i], 16)
            for i, n in enumerate(TOKS):
                sp.wait_ge(s_fo, i + 1)
                sp.dma_start(t["y_out"][P * i:P * i + n, :], fx[i][0:n]).then_inc(s_fst, 16)
            sp.wait_ge(s_fst, 16 * 5)
            sp.wait_ge(s_out, 16 * 4)
            sp.wait_ge(s_kout, 16)
            sp.wait_ge(s_vout, 16)
            sp.wait_ge(s_hst, 16 * 5)

        @block.tensor
        def _(pe):
            mm = pe.matmul

            def product(n, w, rhs, k0, kn, stop=True):
                for kk in range(k0, kn):
                    for h in range(2):
                        last = mm(pair(n)[:, h, :], w(kk), rhs(kk)[:, HALF * h:HALF * (h + 1)],
                                  start=(kk == 0), stop=(kk == kn - 1 and stop))
                return last

            def proj(j, count, freed):
                pe.wait_ge(s_w[j], count)
                if freed is not None:
                    pe.wait_ge(*freed)
                product(j, lambda kk: wring[:, j, kk, :], lambda kk: xg[:, kk, :], 0, 16).then_inc(s_proj, 1)

            pe.wait_ge(s_w[0], 16)
            for c in range(4):
                pe.wait_ge(s_xg[c % 2], c // 2 + 1)
                product(0, lambda kk: wring[:, 0, kk, :], lambda kk: xg[:, kk, :], 4 * c, 4 * c + 4, stop=(c == 3)
                        ).then_inc(s_proj if c == 3 else s_part, 1)
            pe.wait_ge(s_const, 16)
            pe.wait_ge(s_acc, 4)
            for h in range(2):
                last = mm(ps[:, 4 + h, 0:HALF], ones, sq[:, 0, 0, HALF * h:HALF * (h + 1)], start=True, stop=True)
            last.then_inc(s_ss, 1)
            for n in range(1, 8):
                proj(n % 2, 16 * (n // 2 + 1), (s_uev, 3 * (n - 1)) if n >= 2 else None)
            def inject(rd):
                pe.wait_ge(s_bs[rd], 256)
                if rd == 0:
                    pe.wait_ge(s_us, 16 * 20)
                    pe.wait_ge(s_root, 1)
                for b in range(6):
                    g = 6 * rd + b
                    if g >= 4:
                        pe.wait_ge(s_injev, g - 3)
                    for m in range(3 * b, min(3 * b + 3, 16)):
                        ct, r = 4 * (rd % 2) + m // 4, m % 4
                        last = mm(ps[:, 4 + g % 4, 136 * (m - 3 * b):136 * (m - 3 * b + 1)],
                                  bws[rd % 2][:, m // 4, r, :], ust[:, ct, r, :], start=True, stop=True)
                    last.then_inc(s_inj, 1)

            proj(0, 16 * 5, (s_uev, 21))
            proj(1, 16 * 5, (s_uev, 24))
            inject(0)
            inject(1)
            proj(0, 16 * 6, (s_qev, 1))
            proj(1, 16 * 6, (s_qev, 2))
            inject(2)
            inject(3)

            def proj_pairs(a, b):
                with pe.Fori(a, b) as it:
                    for j in range(2):
                        proj(j, it * 16 + 16, (s_qev, it * 2 + (j - 9)))

            proj_pairs(6, 11)
            pe.wait_ge(s_ex, 1)
            pe.wait_ge(s_injev, 24)
            mm(ps[:, 4, 0:DH], smp_p[:, 0:P], ident, start=True, stop=True).then_inc(s_rows, 1)
            proj_pairs(11, 16)
            pe.wait_ge(s_rope, 24)
            pe.wait_ge(s_ku, 8)
            for n in range(8):
                j, hh = n // 2, n % 2
                if n >= 4:
                    pe.wait_ge(s_vrev, n - 3)
                for h in range(4):
                    last = pe.transpose(ps[:, 4 + n % 4, P * h:P * (h + 1)],
                                        v[:, 4 * hh + h, P * j:P * (j + 1)], ident)
                last.then_inc(s_vr, 1)

            def scores(a):
                h, qt = a // 4, a % 4
                if a >= 4:
                    pe.wait_ge(s_msk, a - 3)
                mm(ps[:, qt, 0:P * (qt + 1)], q[:, h, P * qt:P * (qt + 1)], k[:, h, 0:P * (qt + 1)],
                   start=True, stop=True).then_inc(s_sco, 1)

            def turn(a):
                pe.wait_ge(s_p, a + 1)
                if a >= 2:
                    pe.wait_ge(s_ptev, a - 1)
                for j in range(a % 4 + 1):
                    last = pe.transpose(ps[:, 4 + a % 2, P * j:P * (j + 1)], sc[a % 4][:, P * j:P * (j + 1)], ident)
                last.then_inc(s_pt, 1)

            def weigh(h):
                pe.wait_ge(s_ptev, 4 * h + 4)
                if h >= 2:
                    pe.wait_ge(s_oev, h - 1)
                for j in range(4):
                    last = mm(ps[:, 6 + h % 2, P * j:SEQ].rearrange("p (a n) -> p a n", n=P),
                              vrows[:, j, P * h:P * (h + 1)], pt[:, j:4, j, :], start=(j == 0), stop=(j == 3))
                last.then_inc(s_o, 1)

            pe.wait_ge(s_qev, 24)
            for a in range(4):
                scores(a)
            pe.wait_ge(s_vrev, 8)
            for a in range(4 * NH):
                if a + 4 < 4 * NH:
                    scores(a + 4)
                turn(a)
                if a % 4 == 3:
                    weigh(a // 4)
            pe.wait_ge(s_cw, 1)
            pe.wait_ge(s_msk, 4 * NH)
            for i in range(PAIRS):
                r, ct = i % 4, i // 4
                for ri in range(2):
                    last = mm(ps[32 * r:32 * r + 32, ct // 4, P * (ct % 4):P * (ct % 4 + 1)].rearrange(
                        "p (j m) -> p j m", j=CHUNK), bst[:, ri, i, :], cw[:, 0:CHUNK, ri, i, :],
                        start=(ri == 0), stop=(ri == 1))
            last.then_inc(s_lag, 1)
            pe.wait_ge(s_lagd, 1)
            pe.wait_ge(s_state, 1)
            for ct in range(8):
                b = ct % 2
                if ct >= 2:
                    pe.wait_ge(s_z, ct - 1)
                for lag in range(CHUNK):
                    mm(yjc[b][:, lag:CHUNK, :], lagk[:, ct, lag, :], ujc[:, ct, 0:CHUNK - lag, :],
                       start=(lag == 0), stop=False, skip_group_check=True)
                for r in range(4):
                    i = 4 * ct + r
                    for j in range(CHUNK):
                        for ri in range(2):
                            mm(yjc[b][32 * r:32 * r + 32, j, :], cw[:, j + 1, ri, i, :], xs[:, ri, i, 0:NCH],
                               start=False, stop=(j == CHUNK - 1 and ri == 1), skip_group_check=True)
                ys = ps[:, 2 * b + 1, 0:NS]
                mm(ys, lagk[:, ct, 0, :], u[:, ct, SEQ:T], start=True, stop=False, skip_group_check=True)
                for r in range(4):
                    i = 4 * ct + r
                    for ri in range(2):
                        last = mm(ys[32 * r:32 * r + 32, :], cw[:, 1, ri, i, :], x0s[:, ri, i, :],
                                  start=False, stop=(ri == 1), skip_group_check=True)
                last.then_inc(s_y, 1)
                if ct == 0:
                    pe.wait_ge(s_oev, NH)
                    pe.wait_ge(s_ex, 3)
                    for j in range(2):
                        last = mm(ps[:, 6, P * j:P * (j + 1)], smp_ex[j], ident, start=True, stop=True)
                    last.then_inc(s_rows, 1)
                if ct == 1:
                    pe.wait_ge(s_mh, 1)
                    pe.transpose(ps[0:1, 7, 0:P], stat[:, 41:42], ident).then_inc(s_mt, 1)
                if ct == 2:
                    pe.wait_ge(s_mh, 2)
                    mm(ps[:, 6, 0:1], smp_m[0:1, :], ones[0:1, 0:1], start=True, stop=True).then_inc(s_mt, 1)
            pe.wait_ge(s_z, 8)
            pe.wait_ge(s_ptev, 4 * NH)

            def sum_sq(n, squares, done, banks):
                pe.wait_ge(squares, n + 1)
                for h in range(2):
                    last = mm(ps[:, banks + h, 0:HALF], ones, glu_q[:, n % 2, HALF * h:HALF * (h + 1)],
                              start=(n == 0), stop=(n == 7))
                last.then_inc(done, 1)

            for n in range(8):
                pe.wait_ge(s_gw[n % 4], 16 * (n // 4 + 1))
                if n >= 2:
                    pe.wait_ge(s_sig, n - 1)
                gw = glu_w[:, n % 4].rearrange("p (k m) -> p k m", k=8)
                product(n, lambda kk: gw[:, kk, :], lambda kk: u[:, kk, :], 0, 8).then_inc(s_glu, 1)
                if n >= 2:
                    sum_sq(n - 2, s_zsq, s_zss, 4)
                if n == 1:
                    pe.wait_ge(s_spr, 1)
                    mm(ps[0:64, 7, 0:DH + 1], pairs, smp_o, start=True, stop=True).then_inc(s_stp, 1)
                if n == 3:
                    pe.wait_ge(s_spr, 2)
                    pe.transpose(ps[:, 7, 256:320], smp_n[0:64, :], ident[0:64, 0:64]).then_inc(s_stp, 1)
            sum_sq(6, s_zsq, s_zss, 4)
            sum_sq(7, s_zsq, s_zss, 4)

            def rows_of_x2(g):
                pe.wait_ge(s_x2, 4 * g + 4)
                if g == 0:
                    pe.wait_ge(s_gwr, 1)
                for i, n in enumerate(TOKS):
                    b = 5 * g + i
                    if b >= 3:
                        pe.wait_ge(s_trev, b - 2)
                    for m in range(4):
                        last = pe.transpose(ps[0:n, 4 + b % 3, P * m:P * (m + 1)],
                                            x2[:, 4 * g + m, P * i:P * i + n], ident)
                    last.then_inc(s_tr, 1)
                for i, n in enumerate(TOKS):
                    for kk in range(4 * g, 4 * g + 4):
                        last = mm(ps[0:n, 7, 36 * i:36 * (i + 1)], x2[:, kk, P * i:P * i + n], wr[:, kk, :],
                                  start=(kk == 0 and i == 0), stop=(kk == 15), skip_group_check=True)
                if g == 3:
                    last.then_inc(s_lg, 1)

            def outproj(n, k0, kn):
                for kk in range(k0, kn):
                    if n == 0:
                        pe.wait_ge(s_mix, kk + 1)
                    last = product(n, lambda kk: wring[:, n % 2, kk, :],
                                   lambda kk: z2[:, kk, :] if kk < 8 else q[:, kk - 8, :], kk, kk + 1, stop=(kk == 15))
                return last

            pe.wait_ge(s_sig, 8)
            for n in range(2):
                pe.wait_ge(s_w[n % 2], 16 * 17)
                outproj(n, 0, 8)
                if n == 0:
                    pe.wait_ge(s_so, 1)
                for m in range(4 * n, 4 * n + 4):
                    sum_sq(m, s_osq, s_oss, 6)
            for n in range(16):
                if n >= 2:
                    pe.wait_ge(s_w[n % 2], 16 * (16 + n // 2 + 1))
                    pe.wait_ge(s_x2, n - 1)
                outproj(n, 8 if n < 2 else 0, 16).then_inc(s_op, 1)
                if n % 4 == 0 and n:
                    rows_of_x2(n // 4 - 1)
            rows_of_x2(3)
            pe.wait_ge(s_rb, 1)
            for i in range(6):
                for ii in range(min(i, 4) + 1):
                    last = mm(ps[:, 1, 32 * i:32 * (i + 1)], upper16 if ii == i else ones16, m16[:, ii, :],
                              start=(ii == 0), stop=(ii == min(i, 4)))
            last.then_inc(s_pos, 1)
            pe.wait_ge(s_trev, 20)

            def lists(g):
                pe.wait_ge(s_sel, g + 1)
                if g >= 3:
                    pe.wait_ge(s_idx, g - 2)
                for b in range(LISTG):
                    for i in range(5):
                        last = mm(ps[0:CAP, 4 + g % 3, 2 * b:2 * b + 2], sel16[g % 3][:, i, b, :],
                                  rv16[:, i, LISTG * g + b, :], start=(i == 0), stop=(i == 4))
                last.then_inc(s_lst, 1)

            def turn_rows(n, j, it):
                pe.wait_ge(s_gat[j], it * 16 + 16)
                rows = xrow[j][0:CAP, :].rearrange("p (m k) -> p k m", k=16)
                for g in range(4):
                    if not first(n) or g >= 2:
                        pe.wait_ge(s_xte, n * 4 + (g - 1))
                    for m in range(5 * g, min(5 * g + 5, 16)):
                        last = pe.transpose(ps[:, g % 2, CAP * (m - 5 * g):CAP * (m - 5 * g + 1)], rows[:, m, :],
                                            ident[0:CAP, 0:CAP])
                    last.then_inc(s_xt, 1)

            def expert(n, j, it):
                pe.wait_ge(s_e["g"][j], it * 16 + 16)
                pe.wait_ge(s_xte, n * 4 + 4)
                for m in range(4):
                    for kk in range(16):
                        last = mm(ps[:, 2, CAP * m:CAP * (m + 1)], wg[j][:, kk, P * m:P * (m + 1)],
                                  xtr[:, kk, :], start=(kk == 0), stop=(kk == 15))
                last.then_inc(s_ga, 1)
                if first(n):
                    for g in range(3, NBLK // LISTG):
                        lists(g)
                pe.wait_ge(s_e["u"][j], it * 16 + 16)
                for m in range(4):
                    for kk in range(16):
                        last = mm(ps[:, 3, CAP * m:CAP * (m + 1)], wu[j][:, kk, P * m:P * (m + 1)],
                                  xtr[:, kk, :], start=(kk == 0), stop=(kk == 15))
                last.then_inc(s_up, 1)
                turn_rows(n + 1, 1 - j, it + j)
                pe.wait_ge(s_e["d"][0], n * 16 + 16)
                pe.wait_ge(s_ac, n + 1)
                if first(n):
                    pe.wait_ge(s_idx, NBLK // LISTG)
                else:
                    pe.wait_ge(s_yv, n * 4)
                for c in range(4):
                    for kk in range(4):
                        last = mm(ps[0:CAP, 4 + c, :], actt[:, kk, :], wd[:, kk, 512 * c:512 * (c + 1)],
                                  start=(kk == 0), stop=(kk == 3))
                    last.then_inc(s_dn, 1)

            for g in range(3):
                lists(g)
            turn_rows(0, 0, 0)
            blocks(pe, expert)

        @block.scalar
        def _(act):
            A = act.activation
            for c in range(4):
                act.wait_ge(s_x[c], 16)
                if c >= 2:
                    act.wait_ge(s_acc, c - 1)
                A(sq[:, min(c, 1)], xg[:, 4 * c:4 * c + 4, :], ACT.Square).then_inc(s_sq, 1)
                if c % 2 == 0:
                    act.wait_ge(s_gc, 16)
                    act.wait_ge(s_sq, c + 1)
                    for kk in range(4 * c, 4 * c + 4):
                        last = A(xg[:, kk, :], xg[:, kk, :], ACT.Copy, scale=gmix[:, kk:kk + 1])
                    last.then_inc(s_xg[0], 1)
            act.wait_ge(s_set, 1)
            act.wait_ge(s_par, 16)
            A(par[:, 2, :], par[:, 2, :], ACT.Exp).then_inc(s_lact, 1)
            act.wait_ge(s_ldve, 1)
            A(tmp[2], tmp[0], ACT.Exp).then_inc(s_lact, 1)
            act.wait_ge(s_ss, 1)
            A(halves(rstd), ps[:, 4:6, 0:HALF], ACT.Sqrt, bias=eps, scale=1.0 / DM).then_inc(s_root, 1)
            act.wait_ge(s_ldve, 2)
            A(tmp[5], tmp[4], ACT.Sin).then_inc(s_lact, 1)
            A(tmp[6], tmp[4], ACT.Sin, scale=0.5).then_inc(s_lact, 1)
            def stack_weights(rd):
                if rd >= 2:
                    act.wait_ge(s_inj, 6 * (rd - 1))
                for r in range(4):
                    for j in range(CHUNK):
                        act.dma_start(bws[rd % 2][32 * j:32 * j + 32, :, r, :],
                                      bw[32 * r:32 * r + 32, CHUNK - 1 - j, rd // 2, 4 * (rd % 2):4 * (rd % 2) + 4, :]
                                      ).then_inc(s_bs[rd], 16)

            def chunk_states(rd):
                for b in range(6):
                    g, i, n = 6 * rd + b, 16 * (rd % 2) + 3 * b, min(3, 16 - 3 * b)
                    act.wait_ge(s_inj, g + 1)
                    src = ps[:, 4 + g % 4, 0:136 * n].rearrange("p (i n) -> p i n", n=136)
                    A(xs[:, rd // 2, i:i + n, 1:NCH + 1], src[:, :, 0:NCH], ACT.Copy)
                    A(xns[:, rd // 2, i:i + n, :], src[:, :, NCH:136], ACT.Copy).then_inc(s_injev, 1)

            act.wait_ge(s_bw, 1)
            act.wait_ge(s_ldve, 4)
            stack_weights(0)
            stack_weights(1)
            act.wait_ge(s_uev, 24)
            act.wait_ge(s_zu, 1)
            for r in range(4):
                for j in range(CHUNK):
                    act.dma_start(ust[32 * j:32 * j + 32, :, r, 0:NCH], ujc[32 * r:32 * r + 32, :, j, :]).then_inc(s_us, 16)
                act.dma_start(ust[96:128, :, r, NCH:136], u[32 * r:32 * r + 32, :, SEQ:T]).then_inc(s_us, 16)

            for m in range(24):
                if m == 2:
                    chunk_states(2)
                    chunk_states(3)
                act.wait_ge(s_proj, m + 9)
                if m >= 2:
                    act.wait_ge(s_rope, m - 1)
                if m < 16:
                    A(halves(rope_in[0:64, m % 2, 1]), pair(m)[64:128], ACT.Copy)
                    A(halves(rope_in[64:128, m % 2, 1]), pair(m)[0:64], ACT.Copy)
                A(halves(rope_in[:, m % 2, 0]), pair(m), ACT.Copy).then_inc(s_qev, 1)
                if m == 1:
                    for rd in range(2):
                        chunk_states(rd)
                        stack_weights(rd + 2)
            for n in range(8):
                act.wait_ge(s_vr, n + 1)
                if n == 0:
                    act.wait_ge(s_proj, 32)
                A(vrows[:, n // 2, 512 * (n % 2):512 * (n % 2 + 1)], ps[:, 4 + n % 4, :], ACT.Copy).then_inc(s_vrev, 1)

            def exps(a):
                act.wait_ge(s_mx, a + 1)
                w = P * (a % 4 + 1)
                A(sc[a % 4][:, 0:w], sc[a % 4][:, 0:w], ACT.Exp, bias=stat[:, a:a + 1], scale=SCALE).then_inc(s_exp, 1)

            def turned(a):
                act.wait_ge(s_pt, a + 1)
                if a % 4 == 0 and a:
                    act.wait_ge(s_o, a // 4)
                qt = a % 4
                A(pt[:, qt, 0:qt + 1, :], ps[:, 4 + a % 2, 0:P * (qt + 1)].rearrange("p (j n) -> p j n", n=P),
                  ACT.Copy).then_inc(s_ptev, 1)

            def head_out(h):
                act.wait_ge(s_o, h + 1)
                A(q[:, h, 0:SEQ], ps[:, 6 + h % 2, :], ACT.Copy).then_inc(s_oev, 1)

            exps(0)
            for a in range(4 * NH):
                if a + 1 < 4 * NH:
                    exps(a + 1)
                turned(a)
                if a % 4 == 1 and a > 4:
                    head_out(a // 4 - 1)
            head_out(NH - 1)
            act.wait_ge(s_lag, 1)
            act.wait_ge(s_lagc, 1)
            for r in range(4):
                last = A(lagk[32 * r:32 * r + 32, :, :, 32 * r:32 * r + 32],
                         psum_t[32 * r:32 * r + 32, 0:1024].rearrange("p (c j m) -> p c j m", c=8, j=CHUNK), ACT.Copy)
            last.then_inc(s_lagc, 1)
            for ct in range(8):
                act.wait_ge(s_y, ct + 1)
                if ct == 3:
                    act.wait_ge(s_smx, 1)
                    A(smp_p, smp_p, ACT.Exp, bias=stat[:, 40:41], scale=SCALE).then_inc(s_sexp, 1)
                A(u[:, ct, 0:SEQ].rearrange("p (c j) -> p j c", j=CHUNK), yjc[ct % 2], ACT.Gelu_apprx_tanh)
                A(u[:, ct, SEQ:T], ps[:, 2 * (ct % 2) + 1, 0:NS], ACT.Gelu_apprx_tanh).then_inc(s_z, 1)

            def squares(n, src, ready, count, freed, freed_at, done):
                act.wait_ge(ready, count)
                if freed_at > 0:
                    act.wait_ge(freed, freed_at)
                A(glu_q[:, n % 2], src[:, n, :], ACT.Square).then_inc(done, 1)

            for n in range(8):
                act.wait_ge(s_glu, n + 1)
                if n >= 2:
                    act.wait_ge(s_z2, n - 1)
                A(halves(glu_t[:, n % 2]), pair(n), ACT.Sigmoid).then_inc(s_sig, 1)
                if n >= 1:
                    squares(n - 1, z2, s_z2, n, s_zss, n - 2, s_zsq)
            squares(7, z2, s_z2, 8, s_zss, 6, s_zsq)
            act.wait_ge(s_zss, 8)
            A(halves(rz), ps[:, 4:6, 0:HALF], ACT.Sqrt, bias=eps, scale=1.0 / (8 * P)).then_inc(s_zrt, 1)
            for n in range(8):
                squares(n, q, s_so, 1, s_oss, n - 1, s_osq)
            act.wait_ge(s_oss, 8)
            A(halves(ro), ps[:, 6:8, 0:HALF], ACT.Sqrt, bias=eps, scale=1.0 / (8 * P)).then_inc(s_ort, 1)
            for b in range(20):
                g, i = b // 5, b % 5
                n = TOKS[i]
                part = x2_of[i][0:n, 512 * g:512 * (g + 1)]
                act.wait_ge(s_tr, b + 1)
                A(part, ps[0:n, 4 + b % 3, :], ACT.Copy).then_inc(s_trev, 1)
                act.wait_ge(s_trev, b + 1)
                if b:
                    act.wait_ge(s_rss, b)
                A(rowjunk[0:n], part, ACT.Square, accum_out=row_part[0:n, i, g:g + 1]).then_inc(s_rss, 1)
            act.wait_ge(s_rrs, 1)
            A(row_sum, row_sum, ACT.Sqrt, bias=eps, scale=1.0 / DM).then_inc(s_rrt, 1)
            act.wait_ge(s_rrs, 2)
            act.wait_ge(s_x2st, 16 * 8)
            for i, n in enumerate(TOKS):
                A(x2_of[i][0:n], x2_of[i][0:n], ACT.Copy, scale=row_rstd[0:n, i:i + 1]).then_inc(s_hr, 1)
            act.wait_ge(s_ra, 1)
            A(gexp, gexp, ACT.Exp).then_inc(s_ra, 1)
            act.wait_ge(s_ra, 3)
            A(ex, ex, ACT.Exp).then_inc(s_ra, 1)

            def expert(n, j, it):
                act.wait_ge(s_ga, n + 1)
                if not first(n):
                    act.wait_ge(s_ac, n)
                A(sil, ps[:, 2, 0:4 * CAP], ACT.Silu).then_inc(s_si, 1)
                if not first(n):
                    act.wait_ge(s_sct, n * 16)
                for c in range(4):
                    act.wait_ge(s_dn, n * 4 + (c + 1))
                    A(yrow[0:CAP, 512 * c:512 * (c + 1)], ps[0:CAP, 4 + c, :], ACT.Copy).then_inc(s_yv, 1)

            blocks(act, expert)
            for i, n in enumerate(TOKS):
                act.wait_ge(s_fin, i + 1)
                A(fjunk[0:n], fx[i][0:n], ACT.Square, accum_out=fstat[0:n, 0, i:i + 1]).then_inc(s_fq, 1)
                act.wait_ge(s_fq, i + 1)
                A(fstat[0:n, 0, i:i + 1], fstat[0:n, 0, i:i + 1], ACT.Sqrt, bias=eps[0:n], scale=1.0 / DM
                  ).then_inc(s_fr, 1)

        @block.gpsimd
        def _(pool):
            chain = [0]

            def link(ins):
                chain[0] += 1
                ins.then_inc(s_pool, 1)
                pool.wait_ge(s_pool, chain[0])

            tt = pool.tensor_tensor

            def complex_product(outs, a, b, t, negated=False):
                (ar, ai), (br, bi), (tr, ti) = a, b, t
                s1, s2 = (ALU.add, ALU.subtract) if negated else (ALU.subtract, ALU.add)
                tt(tr, ar, br, ALU.mult)
                link(tt(ti, ai, bi, ALU.mult))
                link(tt(outs[0], tr, ti, s1))
                tt(tr, ai, br, ALU.mult)
                link(tt(ti, ar, bi, ALU.mult))
                link(tt(outs[1], tr, ti, s2))

            pool.wait_ge(s_ldve, 3)
            pool.wait_ge(s_braw, 16)
            flat = [[bw[:, kk, r].rearrange("p c n -> p (c n)") for r in range(2)] for kk in range(CHUNK)]
            two = (tmp[4][:, 0:1024], tmp[5][:, 0:1024])
            complex_product(flat[0], (braw[:, 0], braw[:, 1]), (cre[:, 0:1024], cim[:, 0:1024]), two)
            for kk in range(1, CHUNK):
                complex_product(flat[kk], flat[kk - 1], (lre[:, 0:1024], lim[:, 0:1024]), two)
            tt(two[0][:, 0:1], two[0][:, 0:1], two[0][:, 0:1], ALU.mult).then_inc(s_bw, 1)
            pool.wait_ge(s_rstd, 1)
            pool.wait_ge(s_rc, 16)
            pool.wait_ge(s_bw, 1)
            tt(cosr, cos, rstd, ALU.mult)
            link(tt(sinr, sin, rstd, ALU.mult))
            for m in range(24):
                pool.wait_ge(s_qev, m + 1)
                dst = (q, k, v)[m // 8][:, m % 8, :]
                if m < 16:
                    if m == 0:
                        for rd in range(4):
                            pool.wait_ge(s_bs[rd], 256)
                    tt(rope_t[:, 0], rope_in[:, m % 2, 0], cosr, ALU.mult)
                    link(tt(rope_t[:, 1], rope_in[:, m % 2, 1], sinr, ALU.mult))
                    tt(dst, rope_t[:, 0], rope_t[:, 1], ALU.add).then_inc(s_rope, 1)
                    pool.wait_ge(s_rope, m + 1)
                else:
                    tt(dst, rope_in[:, m % 2, 0], rstd, ALU.mult).then_inc(s_rope, 1)
            pool.wait_ge(s_proj, 32)
            pool.wait_ge(s_rope, 24)
            pool.wait_ge(s_state, 1)
            link(pool.memset(lagk, 0.0))
            pool.wait_ge(s_c, 16 * 3)
            link(pool.tensor_scalar(cw[:, 0, 1], cw[:, 0, 1], -1.0, None, ALU.mult))

            def over(ap):
                return ap.unsqueeze(2).to_broadcast([P, PAIRS, 32])

            lam = (over(lamp[:, 0]), over(lamp[:, 1]))
            for kk in range(1, CHUNK + 1):
                complex_product((cw[:, kk, 0], cw[:, kk, 1]), (cw[:, kk - 1, 0], cw[:, kk - 1, 1]), lam, bt, True)
            tr, ti = bt
            cr, ci = over(coef[:, 0]), over(coef[:, 1])
            tt(tr, bst[:, 0], cr, ALU.mult)
            link(tt(ti, bst[:, 1], ci, ALU.mult))
            link(tt(tr, tr, ti, ALU.subtract))
            link(tt(ti, bst[:, 0], ci, ALU.mult))
            link(pool.tensor_copy(bst[:, 0], tr))
            link(tt(tr, bst[:, 1], cr, ALU.mult))
            tt(bst[:, 1], tr, ti, ALU.add).then_inc(s_cw, 1)
            pool.wait_ge(s_cw, 1)
            pool.memset(stat[:, 63:64], 0.0).then_inc(s_lagc, 1)

            def held():
                pool.sem_inc(s_held, 1)

            def gather(n, j):
                pool.wait_ge(s_ig, n + 1)
                held()
                pool.indirect_dma_start(
                    out=xrow[j][0:CAP, :], out_offset=None, in_=h_rows,
                    in_offset=bass.IndirectOffsetOnAxis(ap=idx_now[0:CAP, j:j + 1], axis=0),
                    bounds_check=T - 1, oob_is_err=False).then_inc(s_gat[j], 16)

            def expert(n, j, it):
                pool.wait_ge(s_xt, n * 4 + 4)
                gather(n + 2, j)
                pool.wait_ge(s_is, n + 1)
                pool.wait_ge(s_yv, n * 4 + 4)
                held()
                pool.indirect_dma_start(
                    out=y_rows, out_offset=bass.IndirectOffsetOnAxis(ap=idx_now[0:CAP, 2 + j:3 + j], axis=0),
                    in_=yrow[0:CAP, :], in_offset=None,
                    bounds_check=2 * T - 1, oob_is_err=False).then_inc(s_sct, 16)

            pool.wait_ge(s_hst, 16 * 5)
            for j in range(2):
                pool.memset(xrow[j], 0.0).then_inc(s_z0, 1)
            pool.wait_ge(s_z0, 2)
            for j in range(2):
                gather(j, j)
            blocks(pool, expert)

        @block.vector
        def _(dve):
            tt, ts, stt = dve.tensor_tensor, dve.tensor_scalar, dve.scalar_tensor_tensor
            chain = [0]

            def link(ins):
                chain[0] += 1
                ins.then_inc(s_dve, 1)
                dve.wait_ge(s_dve, chain[0])

            dve.memset(eps, EPS).then_inc(s_set, 1)
            for c in range(4):
                dve.wait_ge(s_sq, c + 1)
                if c % 2:
                    if c == 1:
                        dve.wait_ge(s_gc, 16)
                    tt(xg[:, 4 * c:4 * c + 4, :], xg[:, 4 * c:4 * c + 4, :],
                       gmix[:, 4 * c:4 * c + 4].unsqueeze(2).to_broadcast([P, 4, T]), ALU.mult).then_inc(s_xg[1], 1)
                if c:
                    tt(sq[:, 0], sq[:, 0], sq[:, 1], ALU.add).then_inc(s_acc, 1)
                    dve.wait_ge(s_acc, c)
            link(tt(sq[:, 0, 0:2], sq[:, 0, 0:2], sq[:, 0, 2:4], ALU.add))
            tt(sq[:, 0, 0], sq[:, 0, 0], sq[:, 0, 1], ALU.add).then_inc(s_acc, 1)

            def u_out(n):
                dve.wait_ge(s_proj, n + 1)
                dst = u[:, n, 0:SEQ].rearrange("p (j c) -> p c j", j=CHUNK)
                c0 = HALF // CHUNK

                def src(a, lo, hi):
                    return a[:, lo:hi].rearrange("p (c j) -> p c j", j=CHUNK)

                tt(dst[:, 0:c0], src(pair(n)[:, 0], 0, HALF), src(rstd, 0, HALF), ALU.mult).then_inc(s_uev, 1)
                tt(dst[:, c0:NCH], src(pair(n)[:, 1], 0, SEQ - HALF), src(rstd, HALF, SEQ), ALU.mult).then_inc(s_uev, 1)
                tt(u[:, n, SEQ:T], pair(n)[:, 1, SEQ - HALF:HALF], rstd[:, SEQ:T], ALU.mult).then_inc(s_uev, 1)

            ar, ai, dt = par[:, 0], par[:, 1], par[:, 2]
            dve.wait_ge(s_lact, 1)
            tt(tmp[0], ar, dt, ALU.mult).then_inc(s_ldve, 1)
            link(tt(tmp[1], ai, dt, ALU.mult))
            link(ts(tmp[3], tmp[1], 0.5 / PI, MAGIC, ALU.mult, ALU.add))
            link(ts(tmp[3], tmp[3], MAGIC, None, ALU.subtract))
            link(stt(tmp[4], tmp[3], -TWO_PI[0], tmp[1], ALU.mult, ALU.add))
            link(stt(tmp[4], tmp[3], -TWO_PI[1], tmp[4], ALU.mult, ALU.add))
            link(stt(tmp[4], tmp[3], -TWO_PI[2], tmp[4], ALU.mult, ALU.add))
            ts(tmp[4], tmp[4], 3.1415925, -3.1415925, ALU.min, ALU.max).then_inc(s_ldve, 1)
            dve.wait_ge(s_root, 1)
            dve.reciprocal(rstd, rstd).then_inc(s_rstd, 1)
            dve.wait_ge(s_rstd, 1)
            u_out(0)
            link(tt(tmp[8], ar, ar, ALU.mult))
            link(tt(tmp[9], ai, ai, ALU.mult))
            link(tt(tmp[8], tmp[8], tmp[9], ALU.add))
            link(dve.reciprocal(tmp[9], tmp[8]))
            u_out(1)
            dve.wait_ge(s_lact, 4)
            link(tt(tmp[6], tmp[6], tmp[6], ALU.mult))
            link(ts(tmp[6], tmp[6], -2.0, 1.0, ALU.mult, ALU.add))
            tt(lre, tmp[2], tmp[6], ALU.mult)
            link(tt(lim, tmp[2], tmp[5], ALU.mult))
            link(ts(tmp[7], lre, 1.0, None, ALU.subtract))
            tt(tmp[2], tmp[7], ar, ALU.mult)
            link(tt(tmp[3], lim, ai, ALU.mult))
            link(tt(tmp[2], tmp[2], tmp[3], ALU.add))
            tt(cre, tmp[2], tmp[9], ALU.mult)
            tt(tmp[4], tmp[7], ai, ALU.mult)
            link(tt(tmp[3], lim, ar, ALU.mult))
            link(tt(tmp[3], tmp[3], tmp[4], ALU.subtract))
            tt(cim, tmp[3], tmp[9], ALU.mult).then_inc(s_ldve, 1)
            dve.wait_ge(s_ldve, 3)
            for n in range(2, 8):
                if n == 7:
                    dve.wait_ge(s_bw, 1)
                    dve.memset(ust[:, :, :, NCH:136], 0.0).then_inc(s_zu, 1)
                u_out(n)
                if n == 2:
                    r1, i1 = lre[:, 1024:NP], lim[:, 1024:NP]
                    dve.tensor_copy(lamp[:, 0], r1)
                    dve.tensor_copy(lamp[:, 1], i1)
                    dve.tensor_copy(coef[:, 0], cre[:, 1024:NP])
                    dve.tensor_copy(coef[:, 1], cim[:, 1024:NP])
                    a, b, c, d = (tmp[8][:, 32 * j:32 * j + 32] for j in range(4))
                    for _ in range(2):
                        tt(a, r1, r1, ALU.mult)
                        link(tt(b, i1, i1, ALU.mult))
                        link(tt(d, r1, i1, ALU.mult))
                        link(tt(c, a, b, ALU.subtract))
                        link(ts(d, d, 2.0, None, ALU.mult))
                        e, f = (tmp[9][:, 32 * j:32 * j + 32] for j in range(2))
                        dve.tensor_copy(e, c)
                        link(dve.tensor_copy(f, d))
                        r1, i1 = e, f
                    dve.tensor_copy(lam_same[:, 0], e)
                    dve.tensor_copy(lam_same[:, 1], e)
                    dve.tensor_copy(lam_cross[:, 0], f)
                    ts(lam_cross[:, 1], f, -1.0, None, ALU.mult).then_inc(s_ldve, 1)
            dve.wait_ge(s_bw, 1)
            dve.memset(xs[:, :, :, 0:1], 0.0).then_inc(s_scan, 1)
            dve.wait_ge(s_injev, 24)
            dve.wait_ge(s_ldve, 4)

            def column(c):
                return xs[:, :, :, bass.ds(c, 1)].rearrange("p r i o -> p r (i o)")

            with dve.Fori(0, NCH // 4) as it:
                for s in range(4):
                    done = it * 16 + (4 * s + 1)
                    dve.wait_ge(s_scan, done)
                    tt(scan_t[:, 0], column(it * 4 + s), lam_same, ALU.mult).then_inc(s_scan, 1)
                    tt(scan_t[:, 1, ::-1], column(it * 4 + s), lam_cross, ALU.mult).then_inc(s_scan, 1)
                    dve.wait_ge(s_scan, done + 1)
                    tt(scan_t[:, 2], scan_t[:, 0], column(it * 4 + (s + 1)), ALU.add).then_inc(s_scan, 1)
                    dve.wait_ge(s_scan, done + 3)
                    tt(column(it * 4 + (s + 1)), scan_t[:, 2], scan_t[:, 1], ALU.add).then_inc(s_scan, 1)
            dve.wait_ge(s_c, 16)
            r1, i1 = lamp[:, 0], lamp[:, 1]

            def by_sample(ap):
                return ap.unsqueeze(2).to_broadcast([P, PAIRS, NS])

            t0, t1 = scan_s[:, 0], scan_s[:, 1]
            tt(t0[:, 0], x0s[:, 0], by_sample(r1), ALU.mult)
            tt(t0[:, 1], x0s[:, 1], by_sample(r1), ALU.mult)
            tt(t1[:, 0], x0s[:, 1], by_sample(i1), ALU.mult)
            link(tt(t1[:, 1], x0s[:, 0], by_sample(i1), ALU.mult))
            link(tt(xns, xns, t0, ALU.add))
            tt(xns[:, 0], xns[:, 0], t1[:, 0], ALU.subtract)
            link(tt(xns[:, 1], xns[:, 1], t1[:, 1], ALU.add))
            dve.wait_ge(s_scan, 4 * NCH + 1)
            dve.memset(stat, 0.0).then_inc(s_state, 1)
            def sample(ap):
                return ap[:, :, SEQ:T].rearrange("p h b -> p b h")

            def doubled(dst, src):
                return dve.tensor_copy(dst.rearrange("p (b h s) -> p b h s", b=NS, s=2),
                                       src.unsqueeze(3).to_broadcast([P, NS, NH, 2]))

            def over_keys(row):
                return row.unsqueeze(1).to_broadcast([P, 16, DH])

            dve.wait_ge(s_rope, 8)
            doubled(smp_p[:, 0:P], sample(q)).then_inc(s_ex, 1)
            dve.wait_ge(s_rows, 1)
            link(dve.tensor_copy(smp_q, ps[:, 4, 0:DH]))
            for c in range(8):
                dve.wait_ge(s_kch[c % 2], 16 * (c // 2 + 1))
                link(tt(kch[c % 2], kch[c % 2], over_keys(smp_q), ALU.mult))
                dve.tensor_reduce(smp_p[:, 16 * c:16 * (c + 1)], kch[c % 2], X, ALU.add).then_inc(s_ku, 1)
            dve.wait_ge(s_rope, 24)
            dve.tensor_copy(vsamp, sample(v)).then_inc(s_vs, 1)

            def mask(a):
                qt = a % 4
                w = P * (qt + 1)
                dve.wait_ge(s_sco, a + 1)
                if a >= 4:
                    dve.wait_ge(s_pt, a - 3)
                tt(sc[a % 4][:, 0:w], ps[:, qt, 0:w], branch_neg[:, 512 - w:512], ALU.add).then_inc(s_msk, 1)
                dve.wait_ge(s_msk, a + 1)
                link(dve.tensor_reduce(stat[:, a:a + 1], sc[a % 4][:, 0:w], X, ALU.max))
                ts(stat[:, a:a + 1], stat[:, a:a + 1], -SCALE, None, ALU.mult).then_inc(s_mx, 1)

            def weights(a):
                w = P * (a % 4 + 1)
                dve.wait_ge(s_exp, a + 1)
                link(stt(sc[a % 4][:, 0:w], sc[a % 4][:, 0:w], 1.0, branch_n[:, 512 - w:512], ALU.mult, ALU.mult,
                         accum_out=stat[:, 32 + a % 4:33 + a % 4]))
                link(dve.reciprocal(stat[:, 36 + a % 4:37 + a % 4], stat[:, 32 + a % 4:33 + a % 4]))
                ts(sc[a % 4][:, 0:w], sc[a % 4][:, 0:w], stat[:, 36 + a % 4:37 + a % 4], None, ALU.mult).then_inc(s_p, 1)

            dve.wait_ge(s_attc, 16)
            dve.wait_ge(s_state, 1)
            mask(0)
            mask(1)
            for a in range(4 * NH):
                if a + 2 < 4 * NH:
                    mask(a + 2)
                weights(a)
            dve.wait_ge(s_lagc, 2)
            for ct in range(8):
                last = stt(lagk[:, ct, 0, :], ident, dskip[:, ct:ct + 1], lagk[:, ct, 0, :], ALU.mult, ALU.add)
            last.then_inc(s_lagd, 1)
            dve.wait_ge(s_kout, 16)
            dve.wait_ge(s_o, NH)
            doubled(smp_ex[0], sample(k)).then_inc(s_ex, 1)
            doubled(smp_ex[1], vsamp).then_inc(s_ex, 1)
            dve.wait_ge(s_rows, 2)
            dve.tensor_copy(smp_v, ps[:, 6, P:2 * P])
            link(dve.tensor_copy(smp_k, ps[:, 6, 0:P]))
            link(stt(smp_k, smp_k, 1.0, smp_q, ALU.mult, ALU.mult, accum_out=smp_p[:, HK:HK + 1]))
            dve.tensor_reduce(stat[:, 41:42], smp_p, X, ALU.max).then_inc(s_mh, 1)
            dve.wait_ge(s_mt, 1)
            link(dve.tensor_reduce(smp_n[0:1, 0:64],
                                   ps[0:1, 7, 0:P].rearrange("p (c s) -> p c s", s=2), X, ALU.max))
            dve.tensor_copy(smp_m[0:1].rearrange("p (c s) -> p c s", s=2),
                            smp_n[0:1, 0:64].unsqueeze(2).to_broadcast([1, 64, 2])).then_inc(s_mh, 1)
            dve.wait_ge(s_mt, 2)
            ts(stat[:, 40:41], ps[:, 6, 0:1], -SCALE, None, ALU.mult).then_inc(s_smx, 1)
            dve.wait_ge(s_sexp, 1)
            dve.wait_ge(s_sc, 16)
            link(stt(smp_p, smp_p, 1.0, smp_mult, ALU.mult, ALU.mult, accum_out=smp_o[:, DH:DH + 1]))
            for c in range(8):
                dve.wait_ge(s_vch[c % 2], 16 * (c // 2 + 1))
                link(tt(vch[c % 2], vch[c % 2], over_keys(smp_p[:, 0:HK]), ALU.mult))
                dve.tensor_reduce(smp_o[:, 16 * c:16 * (c + 1)], vch[c % 2], X, ALU.add).then_inc(s_vu, 1)
            dve.wait_ge(s_vu, 8)
            stt(smp_o[:, 0:DH], smp_v, smp_p[:, HK:HK + 1], smp_o[:, 0:DH], ALU.mult, ALU.add).then_inc(s_spr, 1)
            dve.wait_ge(s_rc, 16 * 5)
            dve.memset(row_part, 0.0)
            tt(wr, wr, gffn.unsqueeze(2).to_broadcast([P, 16, 36]), ALU.mult).then_inc(s_gwr, 1)
            dve.wait_ge(s_kout, 16)
            for n in range(8):
                dve.wait_ge(s_sig, n + 1)
                tt(z2[:, n], u[:, n], glu_t[:, n % 2], ALU.mult).then_inc(s_z2, 1)
                if n == 2:
                    dve.wait_ge(s_stp, 1)
                    link(dve.reciprocal(stat[0:64, 42:43], ps[0:64, 7, DH:DH + 1]))
                    ts(smp_n[0:64], ps[0:64, 7, 0:DH], stat[0:64, 42:43], None, ALU.mult).then_inc(s_spr, 1)
                if n == 4:
                    dve.wait_ge(s_stp, 2)
                    dve.tensor_copy(sample(q), ps[:, 7, 256:320].rearrange("p (b h) -> p b h", b=NS)).then_inc(s_so, 1)
            dve.wait_ge(s_zrt, 1)
            link(dve.reciprocal(rz, rz))
            for n in range(8):
                stt(z2[:, n], z2[:, n], gso[:, n:n + 1], rz, ALU.mult, ALU.mult).then_inc(s_mix, 1)
            dve.wait_ge(s_ort, 1)
            link(dve.reciprocal(ro, ro))
            for n in range(8):
                stt(q[:, n], q[:, n], gao[:, n:n + 1], ro, ALU.mult, ALU.mult).then_inc(s_mix, 1)
            dve.wait_ge(s_x2l, 16)
            for n in range(16):
                dve.wait_ge(s_op, n + 1)
                tt(halves(x2[:, n]), pair(n), halves(x2[:, n]), ALU.add).then_inc(s_x2, 1)
            dve.tensor_copy(upper16, region("upper", P))
            dve.memset(ones16, 1.0)
            dve.wait_ge(s_rss, 20)
            dve.tensor_reduce(row_sum, row_part, X, ALU.add).then_inc(s_rrs, 1)
            link(dve.memset(logit, 0.0))
            dve.wait_ge(s_rrt, 1)
            dve.reciprocal(row_rstd, row_sum).then_inc(s_rrs, 1)
            dve.wait_ge(s_rrs, 2)
            dve.wait_ge(s_lg, 1)
            for i, n in enumerate(TOKS):
                last = stt(logit[0:n, i, :], ps[0:n, 7, 36 * i:36 * (i + 1)], row_rstd[0:n, i:i + 1], rbias[0:n],
                           ALU.mult, ALU.add)
            link(last)

            def full(ap, n):
                return ap.unsqueeze(2).to_broadcast([P, 5, n])

            def every(ap, n):
                return ap.unsqueeze(1).to_broadcast([P, 5, n])

            def first_max(src, n, m, lower, index, hot):
                link(dve.tensor_reduce(m, src, X, ALU.max))
                link(tt(lower, src, full(m, n), ALU.is_lt))
                link(stt(lower, lower, 1000.0, every(iota_b[:, 0:n], n), ALU.mult, ALU.add))
                link(dve.tensor_reduce(index, lower, X, ALU.min))
                link(tt(hot, every(iota_b[:, 0:n], n), full(index, n), ALU.is_equal))

            e1, e2, hot1, hot2 = chosen[:, 0:5], chosen[:, 5:10], hot[:, 0:5], hot[:, 5:10]
            lg = logit[:, :, 0:NG]
            first_max(lg, NG, gmax, glow, gidx, ghot)
            tt(gexp, lg, full(gmax, NG), ALU.subtract).then_inc(s_ra, 1)
            link(ts(gmask, ghot, 1e30, -1e30, ALU.mult, ALU.add))
            link(tt(in_group.rearrange("p t (g e) -> p t g e", g=NG),
                    logit[:, :, NG:].rearrange("p t (g e) -> p t g e", g=NG),
                    gmask.unsqueeze(3).to_broadcast([P, 5, NG, EPG]), ALU.add))
            first_max(in_group, NE, m1, elow, e1, hot1)
            link(stt(rest, hot1, -1e33, in_group, ALU.mult, ALU.add))
            first_max(rest, NE, m2, elow2, e2, hot2)
            tt(ex, m2, m1, ALU.subtract).then_inc(s_ra, 1)
            tt(hot1, hot1, full(valid, NE), ALU.mult)
            link(tt(hot2, hot2, full(valid, NE), ALU.mult))
            tt(m16, hot1, hot2, ALU.add).then_inc(s_rb, 1)
            p_, b_, w_, o_, id_ = C10
            ts(id_[:, 0:5], tok, 2.0, 1.0, ALU.mult, ALU.add)
            ts(id_[:, 5:10], tok, 2.0, 2.0, ALU.mult, ALU.add)
            ts(tok1, tok, 1.0, None, ALU.add)
            link(dve.memset(idx_g[:, NBLK:NBLK + 2], int(BIG) - 1))
            dve.wait_ge(s_pos, 1)
            link(dve.tensor_copy(rank, ps[:, 1, 0:160].rearrange("p (t e) -> p t e", t=5)))
            link(dve.tensor_copy(cnt, ps[:, 1, 160:192]))
            link(ts(more_of, cnt, 1.0 / CAP, -0.5 / CAP - 0.5, ALU.mult, ALU.add))
            link(ts(more_of, more_of, MAGIC, None, ALU.add))
            link(ts(more_of, more_of, MAGIC, 0.0, ALU.subtract, ALU.max))
            link(dve.tensor_tensor_scan(upto, ones[:, 0:NE], more_of, 0.0, ALU.mult, ALU.add))
            link(tt(base, upto, more_of, ALU.subtract))

            def both(ap):
                return ap.unsqueeze(1).to_broadcast([P, 2, 5])

            def by_choice(ap):
                return ap.rearrange("p (j t) -> p j t", j=2)

            def over(ap, n):
                return ap.unsqueeze(2).to_broadcast([P, 10, n])

            tt(wide_e[0].rearrange("p (j t) e -> p j t e", j=2), hot.rearrange("p (j t) e -> p j t e", j=2),
               rank.unsqueeze(1).to_broadcast([P, 2, 5, NE]), ALU.mult)
            link(tt(wide_e[1], hot, base.unsqueeze(1).to_broadcast([P, 10, NE]), ALU.mult))
            dve.tensor_reduce(p_, wide_e[0], X, ALU.add)
            link(dve.tensor_reduce(o_, wide_e[1], X, ALU.add))
            link(ts(b_, p_, 1.0 / CAP, 0.5 / CAP - 0.5, ALU.mult, ALU.add))
            link(ts(b_, b_, MAGIC, None, ALU.add))
            link(ts(b_, b_, MAGIC, None, ALU.subtract))
            tt(o_, o_, b_, ALU.add)
            link(stt(w_, b_, -float(CAP), p_, ALU.mult, ALU.add))
            link(stt(o_, o_, float(NE - 1), chosen, ALU.add, ALU.subtract))
            link(stt(o_, b_, 1.0, o_, ALU.min, ALU.mult))
            tt(o_, o_, chosen, ALU.add)
            link(stt(by_choice(w_), by_choice(w_), 1.0, both(valid), ALU.add, ALU.mult))
            link(tt(wide_b[0], iota_b.unsqueeze(1).to_broadcast([P, 10, NBLK]), over(o_, NBLK), ALU.is_equal))
            link(tt(wide_b[1], wide_b[0], over(w_, NBLK), ALU.mult))
            tt(posblk, wide_b[1][:, 0:5], wide_b[1][:, 5:10], ALU.add)
            link(tt(wide_b[0], wide_b[0], over(id_, NBLK), ALU.mult))
            tt(rv16[:, :, :, 0:1], wide_b[0][:, 0:5].unsqueeze(3), wide_b[0][:, 5:10].unsqueeze(3), ALU.add)
            link(dve.tensor_copy(rv16[:, :, :, 1:2], full(tok1, NBLK).unsqueeze(3)))
            LG = NBLK // LISTG

            def select(g):
                if g == 2:
                    dve.wait_ge(s_hst, 16 * 5)
                if g >= 3:
                    dve.wait_ge(s_lst, g - 2)
                tt(sel16[g % 3], iota_s.unsqueeze(1).unsqueeze(1).to_broadcast([P, 5, LISTG, CAP]),
                   posblk[:, :, LISTG * g:LISTG * (g + 1)].unsqueeze(3).to_broadcast([P, 5, LISTG, CAP]),
                   ALU.is_equal).then_inc(s_sel, 1)

            def lists(g):
                dve.wait_ge(s_lst, g + 1)
                src = ps[0:CAP, 4 + g % 3, 0:2 * LISTG].rearrange("p (b c) -> p b c", c=2)
                no = none[0:CAP].rearrange("p (b c) -> p b c", c=2)
                link(ts(no, src, 0.0, BIG, ALU.is_equal, ALU.mult))
                stt(idx_s[0:CAP, LISTG * g:LISTG * (g + 1)].unsqueeze(2), src[:, :, 0:1], -1.0, no[:, :, 0:1],
                    ALU.add, ALU.add)
                stt(idx_g[0:CAP, LISTG * g:LISTG * (g + 1)].unsqueeze(2), src[:, :, 1:2], -1.0, no[:, :, 1:2],
                    ALU.add, ALU.add).then_inc(s_idx, 1)
                dve.wait_ge(s_idx, g + 1)

            def rows_turned(n):
                for g in range(4):
                    dve.wait_ge(s_xt, n * 4 + (g + 1))
                    w = min(5, 16 - 5 * g)
                    tt(xtr[:, 5 * g:5 * g + w, :], ps[:, g % 2, 0:CAP * w].rearrange("p (k n) -> p k n", n=CAP),
                       gtab[:, 5 * g:5 * g + w].unsqueeze(2).to_broadcast([P, w, CAP]), ALU.mult).then_inc(s_xte, 1)

            select(0)
            lists(0)
            for j in range(2):
                dve.tensor_copy(idx_now[0:CAP, j:j + 1], idx_g[0:CAP, j:j + 1]).then_inc(s_ig, 1)
            select(1)
            select(2)
            lists(1)
            lists(2)
            dve.wait_ge(s_gt, 16)
            rows_turned(0)
            dve.wait_ge(s_ra, 4)
            link(dve.tensor_reduce(gsum, gexp, X, ALU.add))
            link(dve.reciprocal(gate1, gsum))
            link(ts(ex_sum, ex, 1.0, None, ALU.add))
            link(dve.reciprocal(gate_1st, ex_sum))
            link(tt(gate_w[:, :, 0:1], gate1.unsqueeze(2), gate_1st.unsqueeze(2), ALU.mult))
            link(tt(gate_w[:, :, 1:2], gate_w[:, :, 0:1], ex.unsqueeze(2), ALU.mult))
            io = iota_b[:, 0:NOV].unsqueeze(2).to_broadcast([P, NOV, NE])
            ot = [ovt, ovt2]
            link(tt(ot[0], base.unsqueeze(1).to_broadcast([P, NOV, NE]), io, ALU.is_le))
            link(tt(ot[1], upto.unsqueeze(1).to_broadcast([P, NOV, NE]), io, ALU.is_gt))
            link(tt(ot[0], ot[0], ot[1], ALU.mult))
            link(tt(ot[0], ot[0], iota_b[:, 0:NE].unsqueeze(1).to_broadcast([P, NOV, NE]), ALU.mult))
            link(dve.tensor_reduce(ovexp, ot[0], X, ALU.add))
            dve.tensor_copy(ovexp_i[:, 0:NOV], ovexp)
            link(dve.tensor_copy(ovexp_i[:, NOV:NOV + 1], upto[:, NE - 1:NE]))
            for g in range(3, LG):
                select(g)
            for g in range(3, LG):
                lists(g)

            def expert(n, j, it):
                dve.wait_ge(s_gat[j], it * 16 + 16)
                dve.tensor_copy(idx_now[0:CAP, j:j + 1], idx_g[0:CAP, bass.ds(n + 2, 1)]).then_inc(s_ig, 1)
                if type(n) is not int:
                    dve.wait_ge(s_sct, n * 16 - 16)
                dve.tensor_copy(idx_now[0:CAP, 2 + j:3 + j], idx_s[0:CAP, bass.ds(n, 1)]).then_inc(s_is, 1)
                dve.wait_ge(s_si, n + 1)
                dve.wait_ge(s_up, n + 1)
                tt(actt.rearrange("p m n -> p (m n)"), sil, ps[:, 3, 0:4 * CAP], ALU.mult).then_inc(s_ac, 1)
                rows_turned(n + 1)

            blocks(dve, expert)
            dve.wait_ge(s_gf, 16)

            def norm(i, n):
                dve.wait_ge(s_fr, i + 1)
                link(dve.reciprocal(fstat[0:n, 1, i:i + 1], fstat[0:n, 0, i:i + 1]))
                stt(fx[i][0:n], fx[i][0:n], fstat[0:n, 1, i:i + 1], fg[0:n], ALU.mult, ALU.mult).then_inc(s_fo, 1)

            for i, n in enumerate(TOKS):
                dve.wait_ge(s_finl[i], 32)
                link(stt(fx[i][0:n], fy[i][0:n, 0, :], gate_w[0:n, i, 0:1], fx[i][0:n], ALU.mult, ALU.add))
                stt(fx[i][0:n], fy[i][0:n, 1, :], gate_w[0:n, i, 1:2], fx[i][0:n], ALU.mult, ALU.add).then_inc(s_fin, 1)
                if i:
                    norm(i - 1, TOKS[i - 1])
            norm(4, NS)


def key_positions(past):
    import numpy as np
    dist = [d for d in range(1, past + 1)
            if d <= 128 or (d % 4 == 0 and d <= 512) or (d % 16 == 0 and d <= 2048)]
    many = [(d <= 128) + (d % 4 == 0 and d <= 512) + (d % 16 == 0 and d <= 2048) for d in dist]
    assert len(dist) == KEYS
    return past - np.array(dist), np.array(many + [3], np.float32)


def constants():
    import numpy as np
    c = {}
    c["c_mats"] = np.concatenate([np.eye(P), np.ones((P, P))], 1).astype(np.float32)
    c["c_upper"] = np.triu(np.ones((P, P)), 1).astype(np.float32)
    half = DH // 2
    pos = np.concatenate([np.arange(SEQ), np.full(NS, 1024)]).astype(np.float32)
    inv = np.float32(10000.0) ** (-np.arange(half, dtype=np.float32) / np.float32(half))
    ang = (pos[:, None] * inv[None, :].astype(np.float32)).astype(np.float32).astype(np.float64)
    cs, sn = np.cos(ang).T, np.sin(ang).T
    c["c_rope"] = np.concatenate([np.concatenate([cs, cs]), np.concatenate([-sn, sn])], 1).astype(np.float32)
    d = (P * np.arange(3, -1, -1)[:, None, None] + np.arange(P)[None, :, None] - np.arange(P)[None, None, :])
    many = ((d >= 0) & (d <= 128)).astype(np.float32)
    for w, s in ((512, 4), (2048, 16)):
        many += (d >= 0) & (d <= w) & (d % s == 0)
    many = many.transpose(1, 0, 2).reshape(P, 512)
    c["c_branch"] = np.concatenate([many, np.where(many > 0, 0.0, -1e30)], 1).astype(np.float32)
    many = key_positions(1024)[1]
    halves = np.concatenate([many[:-1].reshape(2, -1), [[many[-1]], [0]]], 1)
    c["c_sample"] = np.concatenate([np.tile(halves, (64, 1)), np.repeat(np.eye(64), 2, 0)], 1).astype(np.float32)
    tok = P * np.arange(5)[None, :] + np.arange(P)[:, None]
    c["c_router"] = np.concatenate([np.tile(np.arange(NBLK), (P, 1)), np.tile(np.arange(1, CAP + 1), (P, 1)),
                                    tok < T, np.minimum(tok, T)], 1).astype(np.float32)
    return c


def host_inputs(a):
    import numpy as np
    d = constants()
    x = np.concatenate([a["x_prompt"][0], a["x_sample"][:, 0]], 0)
    d["x_cols"] = x.T.reshape(16, P, T).transpose(1, 0, 2)
    d["w_in"] = a["w_in"][0].reshape(16, P, 32, P).transpose(2, 1, 0, 3).reshape(32, P, DM)
    d["w_glu"] = a["w_glu"][0].reshape(8, P, 8, P).transpose(2, 1, 0, 3).reshape(8, P, 1024)
    d["w_out"] = a["w_out"][0].reshape(16, P, 16, P).transpose(2, 1, 0, 3).reshape(16, P, DM)
    g, n, p = 64, 64, 16
    cols = lambda v: v.reshape(-1, P).T
    d["g_cols"] = np.concatenate([cols(a["g_mix_norm"][0]), cols(a["g_ssm_out"][0]), cols(a["g_attn_out"][0]),
                                  cols(a["g_ffn_norm"][0]), cols(a["ssm_d"][0].reshape(-1))], 1)
    par = []
    for v in (a["ssm_a_re"][0], a["ssm_a_im"][0], np.broadcast_to(a["ssm_log_dt"][0][:, None], (g, n))):
        chan = v.reshape(8, 4, 2 * n).transpose(1, 0, 2)
        chan = np.repeat(chan[:, None], 32, 1).reshape(P, 1024)
        par.append(np.concatenate([chan, v.reshape(PAIRS, 2 * n).T], 1))
    d["ssm_par"] = np.stack(par, 1)

    def chan_blocks(b):
        out = np.zeros((4, 2, p, 8, 2, n), np.float32)
        b = b.reshape(8, 4, 2, n, p)
        for s in range(2):
            out[:, s, :, :, s, :] = b[:, :, s].transpose(1, 3, 0, 2)
        return out.reshape(P, 1024)

    def state_blocks(b):
        out = np.zeros((2, n, PAIRS, 2, p), np.float32)
        b = b.reshape(PAIRS, 2, n, p)
        for s in range(2):
            out[s, :, :, s] = b[:, s].transpose(1, 0, 2)
        return out.reshape(P, PAIRS, 32)

    d["ssm_b_chan"] = np.stack([chan_blocks(a["ssm_b_re"][0]), chan_blocks(a["ssm_b_im"][0])], 1)
    d["ssm_b_state"] = np.stack([state_blocks(a["ssm_b_re"][0]), state_blocks(a["ssm_b_im"][0])], 1)
    d["ssm_c"] = np.stack([state_blocks(a["ssm_c_re"][0].transpose(0, 2, 1)),
                           state_blocks(a["ssm_c_im"][0].transpose(0, 2, 1))], 1)
    st = lambda s: s[0].reshape(NS, PAIRS, P).transpose(2, 1, 0)
    d["ssm_x0"] = np.stack([st(a["state_ssm_re"]), st(a["state_ssm_im"])], 1)
    rows = key_positions(a["cache_k"].shape[2])[0]
    ck, cv = a["cache_k"][0][:, rows], a["cache_v"][0][:, rows]
    d["k_cache"] = ck.reshape(NS, 2, 8, 16, NH, DH).transpose(2, 0, 4, 1, 3, 5).reshape(8, P, DM)
    d["v_cache"] = cv.reshape(NS, 2, P, NH, 8, 16).transpose(4, 0, 3, 1, 5, 2).reshape(8, P, DM)
    wr = np.concatenate([a["w_router_group"][0], a["w_router_expert"][0].reshape(DM, NE)], 1)
    d["w_router"] = wr.reshape(16, P, 36).transpose(1, 0, 2).reshape(P, 576)
    d["b_router"] = np.concatenate([a["b_router_group"][0], a["b_router_expert"][0].reshape(-1)])[None]
    d["g_ffn"], d["g_final"] = a["g_ffn_norm"], a["g_final"][None]
    d["w_gate"], d["w_up"], d["w_down"] = a["w_expert_gate"][0], a["w_expert_up"][0], a["w_expert_down"][0]
    return {f"{k}_in": np.ascontiguousarray(v) for k, v in d.items()}


OUTS = {"y_out": (T, DM), "k_out": (P, NH, T), "v_out": (P, NH, T), "state_out": (P, 2, PAIRS, 9)}


def kernel(**inputs):
    import numpy as np
    import concourse.bacc as bacc
    from concourse.bass_utils import run_bass_kernel_spmd
    arrays = host_inputs({name: np.asarray(v) for name, v in inputs.items()})
    nc = bacc.Bacc("TRN2", target_bir_lowering=False, num_devices=1)
    t = {}
    for name, v in arrays.items():
        t[name[:-3]] = nc.dram_tensor(name, v.shape, F32, kind="ExternalInput").ap()
    for name, shape in OUTS.items():
        t[name] = nc.dram_tensor(name, shape, F32, kind="ExternalOutput").ap()
    build(nc, t)
    r = run_bass_kernel_spmd(nc, [arrays], core_ids=[0]).results[0]
    y = r["y_out"]
    kv = []
    for name in ("k_out", "v_out"):
        m = np.asarray(r[name]).transpose(2, 1, 0)
        kv.append((m[:SEQ][None, None], m[SEQ:][None, :, None]))
    states = np.asarray(r["state_out"]).transpose(3, 1, 2, 0).reshape(9, 2, 64, 64)
    return (y[:SEQ][None], y[SEQ:][:, None], kv[0][0], kv[1][0], states[0:1, 0][None], states[0:1, 1][None],
            kv[0][1], kv[1][1], states[1:, 0][None], states[1:, 1][None])
```
